# Optimizing a Trainium2 kernel written in Bass

```python
import jax, jax.numpy as jnp
from jax import lax
import numpy as np

D_MODEL = 1024
BATCH = 1
SEQ = 512
DEPTH = 1

N_META = 16
D_RNN = D_MODEL
N_RNN_BLOCKS = 4
RNN_BLOCK = D_RNN // N_RNN_BLOCKS
CONV_WIDTH = 4
LRU_C = 8.0
POOL_WINDOWS = (2, 4, 8, 16)
N_POOL_GROUPS = len(POOL_WINDOWS)
D_POOL = D_MODEL // 2
POOL_GROUP = D_POOL // N_POOL_GROUPS
N_BRANCH = 2
D_IN_PROJ = 2 * D_RNN + D_POOL + N_BRANCH * D_MODEL
PEER_HEADS = 8
PEER_NKEYS = 128
N_EXPERTS = PEER_NKEYS * PEER_NKEYS
PEER_DK = 256
PEER_HALF = PEER_DK // 2
PEER_TOPK = 16
PEER_TOKENS_PER_STEP = 256
ALPHA = (2.0 * DEPTH) ** 0.25
BETA = (8.0 * DEPTH) ** -0.25
LN_EPS = 1e-5

kernel_name = "hybrid_rglru_pool_peer_deepnorm"

def layer_norm(x, g, b):
    xf = x.astype(jnp.float32)
    mu = jnp.mean(xf, axis=-1, keepdims=True)
    xc = xf - mu
    var = jnp.mean(jnp.square(xc), axis=-1, keepdims=True)
    return xc * lax.rsqrt(var + LN_EPS) * g.astype(jnp.float32) + b.astype(jnp.float32)

def _lru_combine(earlier, later):
    a1, b1 = earlier
    a2, b2 = later
    return a1 * a2, a2 * b1 + b2

def rglru_branch(xr, gate, conv_w, conv_b, w_rg, b_rg, w_ig, b_ig, lru_L):
    B, T, _ = xr.shape
    xc = lax.conv_general_dilated(
        xr.astype(jnp.float32), conv_w.astype(jnp.float32)[:, None, :],
        window_strides=(1,), padding=[(CONV_WIDTH - 1, 0)],
        dimension_numbers=("NWC", "WIO", "NWC"), feature_group_count=D_RNN,
    ) + conv_b
    xb = xc.reshape(B, T, N_RNN_BLOCKS, RNN_BLOCK)
    r = jax.nn.sigmoid(jnp.einsum("btnc,ncd->btnd", xb, w_rg) + b_rg).reshape(B, T, D_RNN)
    i = jax.nn.sigmoid(jnp.einsum("btnc,ncd->btnd", xb, w_ig) + b_ig).reshape(B, T, D_RNN)
    log_a = LRU_C * r * jax.nn.log_sigmoid(lru_L.astype(jnp.float32))
    a = jnp.exp(log_a)
    mult = jnp.sqrt(-jnp.expm1(2.0 * log_a))
    _, h = lax.associative_scan(_lru_combine, (a, mult * i * xc), axis=1)
    return h * jax.nn.gelu(gate.astype(jnp.float32))

def pool_branch(xp, pool_w, pool_scale):
    B, T, _ = xp.shape
    xf = xp.astype(jnp.float32)
    c = jnp.cumsum(xf, axis=1)
    count = jnp.arange(1, T + 1, dtype=jnp.float32)[None, :, None]
    means = []
    for g, w in enumerate(POOL_WINDOWS):
        cg = c[..., g * POOL_GROUP:(g + 1) * POOL_GROUP]
        lag = jnp.pad(cg[:, :-w], ((0, 0), (w, 0), (0, 0)))
        means.append((cg - lag) / jnp.minimum(count, float(w)))
    pooled = jnp.concatenate(means, axis=-1) - xf
    mixed = jnp.einsum("btgc,gcd->btgd", pooled.reshape(B, T, N_POOL_GROUPS, POOL_GROUP), pool_w)
    return mixed.reshape(B, T, D_POOL) * pool_scale

def peer_retrieve(h, w_q, sub_keys):
    N = h.shape[0]
    q = jnp.einsum("nd,de->ne", h, w_q).reshape(N, PEER_HEADS, 2, PEER_HALF)
    s = jnp.einsum("nhpd,hpkd->nhpk", q, sub_keys).astype(jnp.float32)
    sv, si = lax.top_k(s, PEER_TOPK)
    comb = (sv[:, :, 0, :, None] + sv[:, :, 1, None, :]).reshape(N, PEER_HEADS, PEER_TOPK * PEER_TOPK)
    cv, ci = lax.top_k(comb, PEER_TOPK)
    k1 = jnp.take_along_axis(si[:, :, 0], ci // PEER_TOPK, axis=-1)
    k2 = jnp.take_along_axis(si[:, :, 1], ci % PEER_TOPK, axis=-1)
    ids = k1 * PEER_NKEYS + k2
    wts = jax.nn.softmax(cv, axis=-1)
    return ids.reshape(N, PEER_HEADS * PEER_TOPK), wts.reshape(N, PEER_HEADS * PEER_TOPK)

def peer_experts(h, ids, wts, expert_u, expert_v):
    N, D = h.shape
    n_pad = (-N) % PEER_TOKENS_PER_STEP
    hp = jnp.pad(h, ((0, n_pad), (0, 0))).reshape(-1, PEER_TOKENS_PER_STEP, D)
    ip = jnp.pad(ids, ((0, n_pad), (0, 0))).reshape(-1, PEER_TOKENS_PER_STEP, ids.shape[1])
    wp = jnp.pad(wts, ((0, n_pad), (0, 0))).reshape(-1, PEER_TOKENS_PER_STEP, wts.shape[1])

    def step(args):
        hc, ic, wc = args
        u = expert_u[ic]
        z = jax.nn.gelu(jnp.einsum("cd,ced->ce", hc, u).astype(jnp.float32))
        v = expert_v[ic]
        return jnp.einsum("ce,ced->cd", wc * z, v).astype(jnp.float32)

    out = lax.map(step, (hp, ip, wp))
    return out.reshape(-1, D)[:N]

def setup_inputs(seed: int = 0) -> dict:
    key = jax.random.key(seed)
    ks = jax.random.split(key, 26)
    f32 = jnp.float32
    nrm = lambda k, shape, scale: jax.random.normal(k, shape, f32) * scale
    L = DEPTH
    u_a = jax.random.uniform(ks[11], (L, D_RNN), f32, minval=0.9, maxval=0.999)
    a_base = u_a ** (1.0 / LRU_C)
    return {
        "x": nrm(ks[0], (BATCH, SEQ, D_MODEL), 1.0),
        "meta": nrm(ks[1], (N_META, D_MODEL), 1.0),
        "ln_in_g": 1.0 + nrm(ks[2], (D_MODEL,), 0.02),
        "ln_in_b": nrm(ks[3], (D_MODEL,), 0.02),
        "w_in": nrm(ks[4], (L, D_MODEL, D_IN_PROJ), D_MODEL ** -0.5),
        "conv_w": nrm(ks[5], (L, CONV_WIDTH, D_RNN), CONV_WIDTH ** -0.5),
        "conv_b": nrm(ks[6], (L, D_RNN), 0.01),
        "w_rg": nrm(ks[7], (L, N_RNN_BLOCKS, RNN_BLOCK, RNN_BLOCK), RNN_BLOCK ** -0.5),
        "b_rg": nrm(ks[8], (L, N_RNN_BLOCKS, RNN_BLOCK), 0.01),
        "w_ig": nrm(ks[9], (L, N_RNN_BLOCKS, RNN_BLOCK, RNN_BLOCK), RNN_BLOCK ** -0.5),
        "b_ig": nrm(ks[10], (L, N_RNN_BLOCKS, RNN_BLOCK), 0.01),
        "lru_L": jnp.log(a_base) - jnp.log1p(-a_base),
        "w_proj_a": nrm(ks[12], (L, D_RNN, D_MODEL), D_RNN ** -0.5),
        "pool_w": nrm(ks[13], (L, N_POOL_GROUPS, POOL_GROUP, POOL_GROUP), POOL_GROUP ** -0.5),
        "pool_scale": 1.0 + nrm(ks[14], (L, D_POOL), 0.02),
        "w_proj_b": nrm(ks[15], (L, D_POOL, D_MODEL), D_POOL ** -0.5),
        "w_out": nrm(ks[16], (L, D_MODEL, D_MODEL), BETA * D_MODEL ** -0.5),
        "ln1_g": 1.0 + nrm(ks[17], (L, D_MODEL), 0.02),
        "ln1_b": nrm(ks[18], (L, D_MODEL), 0.02),
        "w_q": nrm(ks[19], (L, D_MODEL, PEER_HEADS * PEER_DK), D_MODEL ** -0.5),
        "sub_keys": nrm(ks[20], (L, PEER_HEADS, 2, PEER_NKEYS, PEER_HALF), PEER_HALF ** -0.5),
        "expert_u": nrm(ks[21], (L, N_EXPERTS, D_MODEL), D_MODEL ** -0.5),
        "expert_v": nrm(ks[22], (L, N_EXPERTS, D_MODEL), BETA),
        "ln2_g": 1.0 + nrm(ks[23], (L, D_MODEL), 0.02),
        "ln2_b": nrm(ks[24], (L, D_MODEL), 0.02),
    }

def reference(x, meta, ln_in_g, ln_in_b, w_in, conv_w, conv_b, w_rg, b_rg, w_ig, b_ig, lru_L,
              w_proj_a, pool_w, pool_scale, w_proj_b, w_out, ln1_g, ln1_b, w_q, sub_keys,
              expert_u, expert_v, ln2_g, ln2_b):
    B = x.shape[0]
    meta_b = jnp.broadcast_to(meta[None].astype(x.dtype), (B, N_META, D_MODEL))
    h = layer_norm(jnp.concatenate([meta_b, x], axis=1), ln_in_g, ln_in_b)
    T = h.shape[1]
    for l in range(DEPTH):
        proj = jnp.einsum("btd,de->bte", h, w_in[l])
        xr = proj[..., :D_RNN]
        gate_r = proj[..., D_RNN:2 * D_RNN]
        xp = proj[..., 2 * D_RNN:2 * D_RNN + D_POOL]
        g_logits = proj[..., 2 * D_RNN + D_POOL:]
        y_a = jnp.einsum("bte,ed->btd",
                         rglru_branch(xr, gate_r, conv_w[l], conv_b[l], w_rg[l], b_rg[l],
                                      w_ig[l], b_ig[l], lru_L[l]), w_proj_a[l])
        y_b = jnp.einsum("bte,ed->btd", pool_branch(xp, pool_w[l], pool_scale[l]), w_proj_b[l])
        gates = jax.nn.sigmoid(g_logits.astype(jnp.float32))
        merged = gates[..., :D_MODEL] * y_a + gates[..., D_MODEL:] * y_b
        mix_out = jnp.einsum("btd,de->bte", merged, w_out[l])
        h = layer_norm(ALPHA * h + mix_out, ln1_g[l], ln1_b[l])
        hf = h.reshape(B * T, D_MODEL)
        ids, wts = peer_retrieve(hf, w_q[l], sub_keys[l])
        ffn = peer_experts(hf, ids, wts, expert_u[l], expert_v[l]).reshape(B, T, D_MODEL)
        h = layer_norm(ALPHA * h + ffn, ln2_g[l], ln2_b[l])
    return h[:, N_META:].astype(x.dtype)


_drawn_inputs = setup_inputs


def setup_inputs(seed=0):
    import zlib

    import numpy as np

    out = dict(_drawn_inputs(seed))
    spreads = {}
    factors = {'b_rg': 46.517, 'b_ig': 35.107, 'pool_scale': 3.332, 'ln2_g': 8.487, 'ln2_b': 8.286}
    for name, (base, spread) in spreads.items():
        noise = np.random.default_rng([zlib.crc32(name.encode()), seed]).standard_normal(out[name].shape)
        drawn = base * np.exp(spread * noise) if base else spread * noise
        out[name] = __import__('jax').numpy.asarray(drawn.astype(out[name].dtype))
    for name, factor in factors.items():
        out[name] = (out[name] * factor).astype(out[name].dtype)
    return out
```

```python
from contextlib import ExitStack

import concourse.bass as bass
from concourse import mybir

F32 = mybir.dt.float32
F32R = mybir.dt.float32r
U32 = mybir.dt.uint32
ALU = mybir.AluOpType
ACT = mybir.ActivationFunctionType
AX_X = mybir.AxisListType.X

P = 128
D = 1024
META = 16
N = 512
T = META + N
TH = T // 2
C = D // P
TT = N // P
HD = D // 2
POOL_GROUPS = 4
POOL_C = POOL_GROUPS
CONV = 4
HEADS = 8
KEYS = 128
TOPK = 16
SEL = HEADS * TOPK
ALPHA = 2.0 ** 0.25
EPS = 1e-5
LRU_C = 8.0
GB = 4
GROUPS = KEYS // GB
AHEAD = 4
PRE, BUILD, POST = 8, 4, 8
WT = 32
WCHUNKS = N // WT
SPILL = PRE + BUILD * WCHUNKS // 2 + POST
SPILLED = SPILL // GB
FIRST = AHEAD + SPILLED
NEG = -3.0e38

CW, CB, BR, BI, LL, PSC = 0, 32, 40, 48, 56, 64
NPAR = 68


class Chain:

    def __init__(self, eng, sem):
        self.eng, self.sem, self.base, self.n, self.off = eng, sem, 0, 0, None

    def done(self, ins):
        ins.then_inc(self.sem, 1)
        self.n += 1

    def value(self):
        return self.base + self.n if self.off is None else self.off + self.n

    def wait(self):
        self.eng.wait_ge(self.sem, self.value())

    def enter(self, i, per):
        self.base, self.n, self.per = self.base + self.n, 0, per
        self.off = i * per + self.base

    def leave(self, times):
        assert self.n == self.per, (self.n, self.per)
        self.base, self.n, self.off = self.base + times * self.per, 0, None


def layer(nc, x_d, meta_d, ln_d, par_d, ident_d, iota_d, wxr_d, wxp_d, wga_d, wgl_d, wrgig_d, poolw_d,
          wpa_d, wpb_d, wo_d, wq_d, keys_d, u_d, v_d, out_d):
    w_spill = nc.dram_tensor("w_spill", [WCHUNKS, P, KEYS, WT], F32).ap()
    g_spill = nc.dram_tensor("g_spill", [SPILL, P, N], F32).ap()

    base = (nc.sbuf_base + 63) // 64 * 64
    top = [base]

    def at(name, shape, dt, offset):
        return nc.alloc_sbuf_tensor_at(name, shape, dt, offset=offset)

    def size(shape):
        n = 4
        for s in shape[1:]:
            n *= s
        return n

    def place(name, shape, dt, cursor):
        t = at(name, shape, dt, cursor[0])
        cursor[0] += (size(shape) + 31) // 32 * 32
        assert cursor[0] <= nc.sbuf_usable_end, (name, cursor[0] - nc.sbuf_usable_end)
        return t

    wraw = place("wraw", [P, 2, D], F32, top)
    whi = place("whi", [P, 2, D], F32R, top)
    wlo = place("wlo", [P, 2, D], F32R, top)
    htok = place("htok", [P, TT, D], F32, top)
    ident = place("ident", [P, P], F32, top)
    iota = place("iota", [P, P], F32, top)
    par = place("par", [P, NPAR], F32, top)
    lam = place("lam", [P, 10, C], F32, top)
    stats = place("stats", [P, 5, 12], F32, top)
    mv = place("mv", [P, 5, 2], F32, top)
    veps = place("veps", [P, 5], F32, top)
    sdev = place("sdev", [P, 5], F32, top)
    rstd = place("rstd", [P, 5], F32, top)
    seq = top[0]
    ht_hi = place("ht_hi", [P, C, T], F32R, top)
    ht_lo = place("ht_lo", [P, C, T], F32R, top)
    h1_hi = at("h1_hi", [P, C, N], F32R, seq)
    h1_lo = at("h1_lo", [P, C, N], F32R, seq + size([P, C, N]))
    lnbc_at = nc.sbuf_usable_end // 64 * 64 - 2 * D * 4
    lnbc = at("lnbc", [P, 2, D], F32, lnbc_at)

    region = top[0]
    r = [region]
    R = place("R", [P, C, T], F32, r)
    I = place("I", [P, C, T], F32, r)
    mixed_hi = place("mixed_hi", [P, POOL_C, N], F32R, r)
    mixed_lo = place("mixed_lo", [P, POOL_C, N], F32R, r)
    after_mixed = r[0]
    xrp = place("xrp", [P, 2, CONV - 1 + T], F32, r)
    xc = place("xc", [P, 4, T], F32, r)
    xc_hi = place("xc_hi", [P, 4, T], F32R, r)
    xc_lo = place("xc_lo", [P, 4, T], F32R, r)
    gwraw = place("gwraw", [P, D], F32, r)
    gwhi = place("gwhi", [P, D], F32R, r)
    gwlo = place("gwlo", [P, D], F32R, r)
    xp = place("xp", [P, POOL_C, T], F32, r)
    psa = place("psa", [P, T], F32, r)
    psb = place("psb", [P, T], F32, r)
    pl_hi = place("pl_hi", [P, POOL_C, N], F32R, r)
    hmeta = at("hmeta", [P, D], F32, r[0])
    pl_lo = place("pl_lo", [P, POOL_C, N], F32R, r)
    assert r[0] <= lnbc_at, r[0] - lnbc_at
    r = [after_mixed]
    ya_hi = place("ya_hi", [P, C, N], F32R, r)
    ya_lo = place("ya_lo", [P, C, N], F32R, r)
    after_ya = r[0]
    A = place("A", [P, C, T], F32, r)
    gel = place("gel", [P, 2, N], F32, r)
    yf = place("yf", [P, 2, N], F32, r)
    assert r[0] <= lnbc_at
    r = [region]
    r_g = [after_ya]
    gates = place("gates", [P, 2 * C, N], F32, r_g)
    m1 = place("m1", [P, 2, N], F32, r_g)
    m2 = place("m2", [P, 2, N], F32, r_g)
    assert r_g[0] <= lnbc_at, r_g[0] - lnbc_at
    mg_hi = at("mg_hi", [P, C, N], F32R, region)
    mg_lo = at("mg_lo", [P, C, N], F32R, region + size([P, C, N]))
    assert region + 2 * size([P, C, N]) <= region + 2 * size([P, C, T])
    r = [region + 2 * size([P, C, T])]
    wo_hi = place("wo_hi", [P, C, D], F32R, r)
    wo_lo = place("wo_lo", [P, C, D], F32R, r)
    assert r[0] <= lnbc_at
    r = [region]
    G = place("G", [P, GB * AHEAD, N], F32, r)
    after_g = r[0]
    keys = place("keys", [P, 2 * HEADS, KEYS], F32, r)
    qf = place("qf", [P, 2, N], F32, r)
    S = place("S", [P, TT, KEYS], F32, r)
    S2 = place("S2", [P, TT, KEYS], F32, r)
    sv = place("sv", [P, 2, TT, TOPK], F32, r)
    si = place("si", [P, 2, TT, TOPK], U32, r)
    comb = place("comb", [P, TT, TOPK, TOPK], F32, r)
    comb2 = place("comb2", [P, TT, TOPK * TOPK], F32, r)
    cv = place("cv", [P, TT, TOPK], F32, r)
    ci = place("ci", [P, TT, TOPK], U32, r)
    cv_all = place("cv_all", [P, TT, HEADS, TOPK], F32, r)
    ci_all = place("ci_all", [P, TT, HEADS, TOPK], U32, r)
    si_all = place("si_all", [P, 2, TT, HEADS, TOPK], F32, r)
    cdiv = place("cdiv", [P, 2, TT * SEL], U32, r)
    cidx = place("cidx", [P, 2, TT * SEL], F32, r)
    sel = place("sel", [P, 3, TT * SEL], F32, r)
    ssum = place("ssum", [P, 2, TT * HEADS], F32, r)
    selT_at = r[0] = max(r[0], after_g + size([P, 2, GB, N]) + 2 * size([P, 2, GB, HD]))
    selT = place("selT", [P, 3, N], F32, r)
    cur = place("cur", [P, 3, 2 * WT], F32, r)
    oh1 = at("oh1", [P, 16, KEYS], F32, after_g)
    oh2 = at("oh2", [P, 16, KEYS], F32, after_g + 8192)
    wst_at = r[0]
    wst = place("wst", [P, 2, KEYS, WT], F32, r)
    S_all = at("S_all", [P, 2 * HEADS, TT, KEYS], F32, wst_at)
    prod = at("prod", [P, TOPK, TT * SEL], F32, wst_at)
    r2 = [after_g]
    alo = place("alo", [P, 2, GB, N], F32R, r2)
    vraw_at = r2[0]
    vraw = place("vraw", [P, 2, GB, HD], F32, r2)
    vhi = place("vhi", [P, 2, GB, HD], F32R, r2)
    assert r2[0] <= selT_at
    vlo = place("vlo", [P, 2, GB, HD], F32R, r2)
    wt = place("wt", [P, 2, WCHUNKS, GB, WT], F32, r2)
    ahi = place("ahi", [P, 2, GB, N], F32R, r2)
    gst = place("gst", [P, 2, N], F32, [max(r[0], r2[0])])
    ln2bc = at("ln2bc", [P, 2, D], F32, vraw_at)

    ctx = ExitStack()
    with ctx:
        ps = ctx.enter_context(nc.psum_tensor("ps", [P, 8, 512], F32))

        def sem(name):
            return ctx.enter_context(nc.semaphore(name))

        consts_in = sem("consts_in")
        ln_in = sem("ln_in")
        ln1_in = sem("ln1_in")
        ln2_in = sem("ln2_in")
        x_in = [sem(f"x_in{t}") for t in range(TT + 1)]
        raw_in = [sem("raw_in0"), sem("raw_in1")]
        raw_free = sem("raw_free")
        tile_hi = sem("tile_hi")
        tile_split = sem("tile_split")
        tile_used = sem("tile_used")
        gw_in = sem("gw_in")
        gw_free = sem("gw_free")
        gw_split = sem("gw_split")
        gw_used = sem("gw_used")
        wo_split = sem("wo_split")
        dve_step = sem("dve_step")
        act_step = sem("act_step")
        apart = sem("apart")
        var_ready = sem("var_ready")
        sd_ready = sem("sd_ready")
        h_ready = sem("h_ready")
        tr_done = sem("tr_done")
        ht_hi_done = sem("ht_hi_done")
        ht_split = sem("ht_split")
        lam_e = sem("lam_e")
        lam_ready = sem("lam_ready")
        x_evac = sem("x_evac")
        conv_done = sem("conv_done")
        xc_hi_done = sem("xc_hi_done")
        xc_split = sem("xc_split")
        ri_done = sem("ri_done")
        ri_evac = sem("ri_evac")
        pooled = sem("pooled")
        pl_hi_done = sem("pl_hi_done")
        pl_split = sem("pl_split")
        mix_done = sem("mix_done")
        mixed_hi_done = sem("mixed_hi_done")
        mixed_split = sem("mixed_split")
        at_done = sem("at_done")
        m_done = sem("m_done")
        mult_done = sem("mult_done")
        gelu_done = sem("gelu_done")
        yf_done = sem("yf_done")
        ya_hi_done = sem("ya_hi_done")
        ya_split = sem("ya_split")
        gl_free = sem("gl_free")
        y_free = sem("y_free")
        mf_done = sem("mf_done")
        mg_hi_done = sem("mg_hi_done")
        mg_split = sem("mg_split")
        o_done = sem("o_done")
        h1_ready = sem("h1_ready")
        tr1_done = sem("tr1_done")
        h1_hi_done = sem("h1_hi_done")
        h1_split = sem("h1_split")
        acc_ready = sem("acc_ready")
        keys_in = sem("keys_in")
        q_free = sem("q_free")
        s_done = sem("s_done")
        s_free = sem("s_free")
        z_free = sem("z_free")
        cmax_ready = sem("cmax_ready")
        cexp_done = sem("cexp_done")
        sel_ready = sem("sel_ready")
        selT_done = sem("selT_done")
        selT_ready = sem("selT_ready")
        oh_ready = sem("oh_ready")
        quad_done = sem("quad_done")
        quad_free = sem("quad_free")
        gst_stored = [sem("gst_stored0"), sem("gst_stored1")]
        g_in = [sem("g_in0"), sem("g_in1")]
        w_stored = [sem("w_stored0"), sem("w_stored1")]
        v_in = [sem("v_in0"), sem("v_in1")]
        vraw_free = [sem("vraw_free0"), sem("vraw_free1")]
        v_hi = sem("v_hi")
        v_split = sem("v_split")
        w_in = [sem("w_in0"), sem("w_in1")]
        w_free = [sem("w_free0"), sem("w_free1")]
        a_ready = sem("a_ready")
        a_hi = sem("a_hi")
        a_split = sem("a_split")
        oe_done = sem("oe_done")
        oe_free = sem("oe_free")
        out_ready = sem("out_ready")
        out_stored = sem("out_stored")

        T_XR, T_XP, T_GA = 0, C, C + POOL_C
        T_GL = T_GA + C
        T_Y = T_GL + 2 * C
        T_Q = T_Y + 2 * C
        T_U = T_Q + 2 * HEADS
        T_US = T_U + GB * AHEAD
        T_UD = T_U + GB * FIRST
        T_END = T_U + KEYS
        RAW_WO = C

        block = ctx.enter_context(nc.Block())

        @block.sync
        def _(sp):
            def load(n, src, cols=D):
                tile, slot = n
                sp.wait_ge(raw_free, tile + 1)
                sp.dma_start(wraw[:, slot, 0:cols], src).then_inc(raw_in[slot], 16)

            def one(d, k):
                return d[bass.ds(k, 1)].rearrange("a p n -> (a p) n")

            sp.dma_start(htok[:, 0, :], x_d[0]).then_inc(x_in[1], 16)
            sp.dma_start(hmeta[0:META, :], meta_d).then_inc(x_in[0], 16)
            for t in range(1, TT):
                sp.dma_start(htok[:, t, :], x_d[t]).then_inc(x_in[t + 1], 16)
            for k in range(2):
                sp.dma_start(lnbc[:, k, :], ln_d[k:k + 1, :].partition_broadcast(P)).then_inc(ln_in, 16)
            sp.dma_start(ident[:, :], ident_d).then_inc(consts_in, 16)
            sp.dma_start(iota[:, :], iota_d).then_inc(consts_in, 16)
            sp.dma_start(par[:, :], par_d).then_inc(consts_in, 16)

            def gate_weights(k):
                sp.wait_ge(gw_free, k + 1)
                if k < 4:
                    sp.dma_start(gwraw[:, :], wrgig_d[k]).then_inc(gw_in, 16)
                else:
                    sp.dma_start(gwraw[:, 0:N], poolw_d).then_inc(gw_in, 16)

            for c in range(C):
                load((T_XR + c, c % 2), wxr_d[c])
                if c % 2 == 1:
                    gate_weights(c // 2)
            for c in range(POOL_C):
                load((T_XP + c, c % 2), wxp_d[c])
            gate_weights(4)
            for c in range(C):
                load((T_GA + c, c % 2), wga_d[c])
            with sp.Fori(0, C) as i:
                for j in range(2):
                    load((i * 2 + (T_GL + j), j), one(wgl_d, i * 2 + j))
            with sp.Fori(0, C) as i:
                load((i * 2 + T_Y, 0), one(wpa_d, i))
                load((i * 2 + (T_Y + 1), 1), one(wpb_d, i), N)
            sp.wait_ge(ht_split, 2 * (TT + 1))
            for k in range(2):
                sp.dma_start(lnbc[:, k, :], ln_d[2 + k:3 + k, :].partition_broadcast(P)).then_inc(ln1_in, 16)
            for c in range(C):
                load((T_Q + c, c % 2), wo_d[c])
            sp.wait_ge(o_done, TT)
            sp.dma_start(keys[:, :, :], keys_d).then_inc(keys_in, 16)
            with sp.Fori(0, HEADS) as i:
                for j in range(2):
                    load((i * 2 + (T_Q + RAW_WO + j), j), one(wq_d, i * 2 + j))
            with sp.Fori(0, GB * AHEAD // 2) as i:
                for j in range(2):
                    load((i * 2 + (T_U + RAW_WO + j), j), one(u_d, i * 2 + j))
            def u_load(b, j):
                load((b + (T_US + RAW_WO), j % 2), one(u_d, b + GB * AHEAD))

            def g_store(b, j):
                sp.wait_ge(z_free, b + (GB * AHEAD + 3))
                sp.dma_start(g_spill[bass.ds(b, 1)].rearrange("a p n -> (a p) n"), gst[:, j % 2, :])\
                    .then_inc(gst_stored[j % 2], 16)

            LOOK = 3
            sp.sem_inc(gst_stored[0], 16)
            sp.sem_inc(gst_stored[1], 16)
            for b in range(LOOK):
                u_load(b, b)
            with sp.Fori(0, PRE // 2) as i:
                for j in range(2):
                    u_load(i * 2 + (j + LOOK), j + LOOK)
                    g_store(i * 2 + j, j)
            sp.sem_inc(w_stored[0], 16)
            sp.sem_inc(w_stored[1], 16)
            with sp.Fori(0, WCHUNKS // 2) as i:
                for s in range(2):
                    for j in range(2):
                        b = 2 * s + j
                        u_load(i * BUILD + (PRE + b + LOOK), b + LOOK)
                        if j == 1:
                            sp.wait_ge(quad_free, i * 16 + (4 + 8 * (s + 1)))
                            sp.dma_start(w_spill[bass.ds(i * 2 + s, 1)].rearrange("a p k t -> (a p) (k t)"),
                                         wst[:, s].rearrange("p k t -> p (k t)")).then_inc(w_stored[s], 16)
                        g_store(i * BUILD + (PRE + b), b)

            def v_load(g, k, dh):
                sp.wait_ge(vraw_free[dh], k + 1)
                sp.dma_start(vraw[:, dh].rearrange("p b n -> p (b n)"),
                             v_d[bass.ds(g * 2 + dh, 1)].rearrange("a p n -> (a p) n")).then_inc(v_in[dh], 16)

            def w_load(g, slot, k):
                sp.wait_ge(w_free[slot], k + 1)
                sp.dma_start(wt[:, slot].rearrange("p c k t -> p c (k t)"),
                             w_spill[:, :, bass.ds(g * GB, GB), :].rearrange("c p k t -> p c (k t)"))\
                    .then_inc(w_in[slot], 16)

            v_load(0, 0, 0)
            v_load(0, 0, 1)
            for b in range(POST):
                if b + LOOK < POST:
                    u_load(SPILL - POST + b + LOOK, b + LOOK)
                g_store(SPILL - POST + b, b)
                if b == 0:
                    sp.wait_ge(w_stored[0], 16 * (WCHUNKS // 2 + 1))
                    sp.wait_ge(w_stored[1], 16 * (WCHUNKS // 2 + 1))
                    w_load(0, 0, 0)
                    w_load(1, 1, 0)
            for j in range(2):
                sp.wait_ge(gst_stored[j], 16 * (SPILL // 2 + 1))

            def g_load(g, slot):
                sp.wait_ge(a_split, g - 1)
                sp.dma_start(G[:, slot * GB:(slot + 1) * GB, :],
                             g_spill[bass.ds((g - AHEAD) * GB, GB)].rearrange("b p n -> p b n"))\
                    .then_inc(g_in[slot], 16)

            for g in range(1, AHEAD):
                w_load(g + 1, (g + 1) % 2, (g + 1) // 2)
                if g + 1 == AHEAD:
                    g_load(g + 1, (g + 1) % 2)
                v_load(g, g, 0)
                v_load(g, g, 1)
            with sp.Fori(0, SPILLED // 2 - 1) as i:
                for s in range(2):
                    g = i * 2 + (AHEAD + s)
                    w_load(i * 2 + (AHEAD + s + 1), (s + 1) % 2, i + (AHEAD + s + 1) // 2)
                    g_load(i * 2 + (AHEAD + s + 1), (s + 1) % 2)
                    v_load(g, g, 0)
                    v_load(g, g, 1)
            for g in (FIRST - 2, FIRST - 1):
                if g + 1 < FIRST:
                    w_load(g + 1, (g + 1) % 2, (g + 1) // 2)
                    g_load(g + 1, (g + 1) % 2)
                v_load(g, g, 0)
                v_load(g, g, 1)
            with sp.Fori(0, (GROUPS - FIRST) // 2) as i:
                for b in range(4):
                    u_load(i * 8 + (SPILL + b), b)
                g = i * 2 + FIRST
                v_load(g, g, 0)
                v_load(g, g, 1)
                w_load(g, 0, i + FIRST // 2)
                w_load(g + 1, 1, i + FIRST // 2)
                u_load(i * 8 + (SPILL + 4), 4)
                u_load(i * 8 + (SPILL + 5), 5)
                v_load(g + 1, g + 1, 0)
                v_load(g + 1, g + 1, 1)
                u_load(i * 8 + (SPILL + 6), 6)
                u_load(i * 8 + (SPILL + 7), 7)
            for k in range(2):
                sp.wait_ge(vraw_free[0], GROUPS + 1)
                sp.dma_start(ln2bc[:, k, :], ln_d[4 + k:5 + k, :].partition_broadcast(P)).then_inc(ln2_in, 16)
            for t in range(TT):
                sp.wait_ge(out_ready, t + 1)
                sp.dma_start(out_d[t], htok[:, t, :]).then_inc(out_stored, 16)
            sp.wait_ge(out_stored, 16 * TT)

        @block.gpsimd
        def _(pool):
            pool.sem_inc(raw_free, 2)
            pool.sem_inc(gw_free, 1)

            def split(raw, hi, lo, ready, free, hi_count):
                nc.gpsimd.tensor_scalar(hi, raw, 1.0, 0.0, ALU.mult, ALU.add).then_inc(tile_hi, 1)
                pool.wait_ge(tile_hi, hi_count)
                nc.gpsimd.tensor_tensor(lo, raw, hi.bitcast(F32), ALU.subtract).then_inc(ready, 1)

            def ring_tile(slot, k_raw, k_ring, hi_count, cols=D):
                pool.wait_ge(raw_in[slot], k_raw)
                pool.wait_ge(tile_used, k_ring)
                pool.sem_inc(apart, 1)
                split(wraw[:, slot, 0:cols], whi[:, slot, 0:cols], wlo[:, slot, 0:cols], tile_split, raw_free, hi_count)
                pool.wait_ge(tile_split, k_ring)
                pool.sem_inc(raw_free, 1)

            def gate_tile(k, hi_count, cols=D):
                pool.wait_ge(gw_in, 16 * (k + 1))
                if k:
                    pool.wait_ge(gw_used, k)
                split(gwraw[:, 0:cols], gwhi[:, 0:cols], gwlo[:, 0:cols], gw_split, gw_free, hi_count)
                pool.wait_ge(gw_split, k + 1)
                pool.sem_inc(gw_free, 1)

            n = 0
            m = 0
            for c in range(C):
                m += 1
                ring_tile(c % 2, 16 * (n // 2 + 1), n + 1, m)
                n += 1
                if c % 2 == 1:
                    m += 1
                    gate_tile(c // 2, m)
            for c in range(POOL_C):
                m += 1
                ring_tile(c % 2, 16 * (n // 2 + 1), n + 1, m)
                n += 1
            m += 1
            gate_tile(4, m, N)
            for c in range(C):
                m += 1
                ring_tile(c % 2, 16 * (n // 2 + 1), n + 1, m)
                n += 1

            def ring_loop(times, n, m, raw_shift, cols=(D, D)):
                with pool.Fori(0, times) as i:
                    for j in range(2):
                        ring_tile(j, i * 16 + 16 * ((n + raw_shift) // 2 + 1), i * 2 + (n + j + 1),
                                  i * 2 + (m + j + 1), cols[j])
                return n + 2 * times, m + 2 * times

            n, m = ring_loop(C, n, m, 0)
            n, m = ring_loop(C, n, m, 0, (D, N))
            assert n == T_Q
            pool.wait_ge(mg_split, C)
            for c in range(C):
                m += 1
                pool.wait_ge(raw_in[c % 2], 16 * ((n + c) // 2 + 1))
                split(wraw[:, c % 2, :], wo_hi[:, c, :], wo_lo[:, c, :], wo_split, raw_free, m)
                pool.wait_ge(wo_split, c + 1)
                pool.sem_inc(raw_free, 1)
            n, m = ring_loop(HEADS, n, m, RAW_WO)
            n, m = ring_loop(GB * AHEAD // 2, n, m, RAW_WO)
            ring_loop((KEYS - GB * AHEAD) // 2, n, m, RAW_WO)

        @block.tensor
        def _(pe):
            pe.sem_inc(tile_used, 2)
            pe.sem_inc(oe_done, 16)

            def three(out, lhi, llo, rhi, rlo, start, stop):
                nc.tensor.matmul(out, lhi, rhi, start=start, stop=False)
                nc.tensor.matmul(out, lhi, rlo, start=False, stop=False)
                return nc.tensor.matmul(out, llo, rhi, start=False, stop=stop)

            def tile_product(slot, outs, rhs, chunks=C):
                for c in range(chunks):
                    w = slice(c * P, (c + 1) * P)
                    for out, cols in outs:
                        mm = three(out, whi[:, slot, w], wlo[:, slot, w], rhs[0][:, c, cols], rhs[1][:, c, cols],
                                   c == 0, c == chunks - 1)
                return mm

            pe.wait_ge(consts_in, 48)
            for t in range(TT + 1):
                pe.wait_ge(h_ready, t + 1)
                rows = META if t == 0 else P
                for hh in range(2):
                    u = 2 * t + hh
                    if u >= 8:
                        pe.wait_ge(ht_split, u - 7)
                    for k in range(4):
                        c = 4 * hh + k
                        s = hmeta[0:META, c * P:(c + 1) * P] if t == 0 else htok[:, t - 1, c * P:(c + 1) * P]
                        mm = nc.tensor.transpose(ps[:, u % 8, k * P:k * P + rows], s, ident[0:rows, 0:rows])
                    mm.then_inc(tr_done, 1)
            pe.wait_ge(ht_split, 2 * (TT + 1))

            def x_chunk(n):
                pe.wait_ge(tile_split, n + 1)
                if n >= 2:
                    pe.wait_ge(x_evac, n - 1)
                b = 2 * (n % 2)
                outs = [(ps[:, b + k, 0:TH], slice(k * TH, (k + 1) * TH)) for k in range(2)]
                tile_product(n % 2, outs, (ht_hi, ht_lo)).then_inc(tile_used, 1)

            def gates_of(n):
                pe.wait_ge(gw_split, n + 1)
                pe.wait_ge(xc_split, 2 * n + 2)
                for o in range(4):
                    k = 4 * n + o
                    if k >= 2:
                        pe.wait_ge(ri_evac, k - 1)
                    b = 4 + 2 * (k % 2)
                    for kc in range(2):
                        w = slice((o // 2) * 512 + kc * 256 + (o % 2) * P, (o // 2) * 512 + kc * 256 + (o % 2) * P + P)
                        x = (2 * n + kc) % 4
                        for half in range(2):
                            cols = slice(half * TH, (half + 1) * TH)
                            mm = three(ps[:, b + half, 0:TH], gwhi[:, w], gwlo[:, w], xc_hi[:, x, cols],
                                       xc_lo[:, x, cols], kc == 0, kc == 1)
                    mm.then_inc(ri_done, 1)
                pe.wait_ge(ri_done, 4 * n + 4)
                pe.sem_inc(gw_used, 1)

            x_chunk(0)
            x_chunk(1)
            for n in range(3):
                x_chunk(2 * n + 2)
                x_chunk(2 * n + 3)
                gates_of(n)
            x_chunk(8)
            x_chunk(9)
            gates_of(3)
            x_chunk(10)
            x_chunk(11)

            def gate_chunk(c):
                pe.wait_ge(tile_split, T_GA + c + 1)
                if c == 0:
                    pe.wait_ge(x_evac, 12)
                if c == 4:
                    pe.wait_ge(mixed_split, 4)
                tile_product(c % 2, [(ps[:, c, :], slice(META, T))], (ht_hi, ht_lo)).then_inc(tile_used, 1)

            gate_chunk(0)
            gate_chunk(1)
            pe.wait_ge(gw_split, 5)
            pe.wait_ge(ri_evac, 16)
            for g in range(POOL_GROUPS):
                pe.wait_ge(pl_split, g + 1)
                three(ps[:, 4 + g, :], gwhi[:, g * P:(g + 1) * P], gwlo[:, g * P:(g + 1) * P],
                      pl_hi[:, g, :], pl_lo[:, g, :], True, True).then_inc(mix_done, 1)
            for c in range(2, C):
                gate_chunk(c)

            pe.wait_ge(gelu_done, 2)
            with pe.Fori(0, C) as i:
                for j in range(2):
                    pe.wait_ge(tile_split, i * 2 + (T_GL + j + 1))
                    pe.wait_ge(gl_free, i * 2 + (j + 1))
                    tile_product(j, [(ps[:, j, :], slice(META, T))], (ht_hi, ht_lo)).then_inc(tile_used, 1)
            pe.wait_ge(gelu_done, C)
            pe.wait_ge(ya_split, C)
            pe.wait_ge(mixed_split, POOL_C)
            with pe.Fori(0, C // 2) as i:
                for j in range(2):
                    pe.wait_ge(y_free, i * 2 + (j + 1))
                    pe.wait_ge(tile_split, i * 4 + (T_Y + 2 * j + 1))
                    tile_product(0, [(ps[:, 2 + j, :], slice(0, N))], (ya_hi, ya_lo)).then_inc(tile_used, 1)
                    pe.wait_ge(tile_split, i * 4 + (T_Y + 2 * j + 2))
                    tile_product(1, [(ps[:, 4 + j, :], slice(0, N))], (mixed_hi, mixed_lo), POOL_C)\
                        .then_inc(tile_used, 1)

            pe.wait_ge(mg_split, C)
            for t in range(TT):
                for c in range(C):
                    if t == 0:
                        pe.wait_ge(wo_split, c + 1)
                    rows = slice(t * P, (t + 1) * P)
                    for dh in range(2):
                        cols = slice(dh * HD, (dh + 1) * HD)
                        mm = three(ps[:, 2 * t + dh, :], mg_hi[:, c, rows], mg_lo[:, c, rows],
                                   wo_hi[:, c, cols], wo_lo[:, c, cols], c == 0, c == C - 1)
                mm.then_inc(o_done, 1)

            def h1_transposes(t):
                pe.wait_ge(h1_ready, t + 1)
                for hh in range(2):
                    for k in range(4):
                        c = 4 * hh + k
                        mm = nc.tensor.transpose(ps[:, 2 * t + hh, k * P:(k + 1) * P],
                                                 htok[:, t, c * P:(c + 1) * P], ident[:, :])
                    mm.then_inc(tr1_done, 1)

            for t in range(TT):
                h1_transposes(t)

            pe.wait_ge(h1_split, 2 * TT)
            pe.wait_ge(keys_in, 16)
            pe.sem_inc(s_done, 2)
            with pe.Fori(0, HEADS) as i:
                for j in range(2):
                    pe.wait_ge(tile_split, i * 2 + (T_Q + j + 1))
                    pe.wait_ge(q_free, i * 2 + (j + 1))
                    tile_product(j, [(ps[:, j, :], slice(0, N))], (h1_hi, h1_lo)).then_inc(tile_used, 1)
                for j in range(2):
                    pe.wait_ge(q_free, i * 2 + (j + 3))
                    pe.wait_ge(s_free, i * 2 + (j + 1))
                    for t in range(TT):
                        mm = nc.tensor.matmul(ps[:, 2 + j, t * KEYS:(t + 1) * KEYS], qf[:, j, t * P:(t + 1) * P],
                                              keys[:, bass.ds(i * 2 + j, 1), :].rearrange("p a k -> p (a k)"),
                                              start=True, stop=True)
                    mm.then_inc(s_done, 1)

            def hidden(slot, bank, tile):
                pe.wait_ge(tile_split, tile + 1)
                tile_product(slot, [(ps[:, bank, :], slice(0, N))], (h1_hi, h1_lo)).then_inc(tile_used, 1)

            with pe.Fori(0, GB * AHEAD // 2) as i:
                for j in range(2):
                    pe.wait_ge(z_free, i * 2 + (j + 1))
                    hidden(j, 4 + j, i * 2 + (T_U + j))

            with pe.Fori(0, PRE // 2) as i:
                for j in range(2):
                    pe.wait_ge(z_free, i * 2 + (GB * AHEAD + j + 1))
                    hidden(j, 4 + j, i * 2 + (T_US + j))

            pe.wait_ge(sel_ready, 1)
            for k in range(3):
                bank = 6 + k if k < 2 else 0
                if k == 2:
                    pe.wait_ge(q_free, 2 + 2 * HEADS)
                for t in range(TT):
                    mm = nc.tensor.transpose(ps[:, bank, t * P:(t + 1) * P], sel[:, k, t * SEL:(t + 1) * SEL],
                                             ident[:, :])
                mm.then_inc(selT_done, 1)

            pe.wait_ge(selT_ready, 3)
            pe.wait_ge(s_free, 2 + 2 * HEADS)
            pe.sem_inc(quad_done, 4)
            with pe.Fori(0, WCHUNKS // 2) as i:
                for s in range(2):
                    for q in range(WT // 4):
                        k = s * 8 + q
                        pe.wait_ge(oh_ready, i * 16 + (k + 2))
                        pe.wait_ge(quad_free, i * 16 + (k + 1))
                        for t in range(4):
                            e = 4 * (q % 4) + t
                            mm = nc.tensor.matmul(ps[:, q % 4, t * P:(t + 1) * P], oh2[:, e, :], oh1[:, e, :],
                                                  start=True, stop=True)
                        mm.then_inc(quad_done, 1)
                        if q % 4 == 3:
                            b = k // 4
                            pe.wait_ge(z_free, i * BUILD + (GB * AHEAD + PRE + b + 1))
                            hidden(b % 2, 4 + b % 2, i * BUILD + (T_US + PRE + b))
            for b in range(SPILL - POST, SPILL):
                pe.wait_ge(z_free, GB * AHEAD + b + 1)
                hidden(b % 2, 4 + b % 2, T_US + b)

            def mix_group(par_, g):
                pe.wait_ge(a_split, g + 1)
                for dh in range(2):
                    pe.wait_ge(v_split, g * 2 + (dh + 1))
                    for t in range(TT):
                        pe.wait_ge(oe_free, g * 8 + (dh * 4 + t + 1))
                        rows = slice(t * P, (t + 1) * P)
                        for b in range(GB):
                            mm = three(ps[:, 4 + t, :], ahi[:, par_, b, rows], alo[:, par_, b, rows],
                                       vhi[:, dh, b, :], vlo[:, dh, b, :], b == 0, b == GB - 1)
                        mm.then_inc(oe_done, 1)

            pe.wait_ge(z_free, 2 + GB * FIRST)
            with pe.Fori(0, FIRST // 2) as i:
                for s in range(2):
                    mix_group(s, i * 2 + s)
            pe.wait_ge(quad_free, 4 + N // 4)
            with pe.Fori(0, (GROUPS - FIRST) // 2) as i:
                for b in range(2 * GB):
                    pe.wait_ge(z_free, i * 8 + (GB * FIRST + b + 1))
                    hidden(b % 2, b % 2, i * 8 + (T_UD + b))
                for s in range(2):
                    mix_group(s, i * 2 + (FIRST + s))

        @block.scalar
        def _(act):
            ch = Chain(act, act_step)
            act.sem_inc(gl_free, 2)
            act.sem_inc(q_free, 2)
            act.sem_inc(s_free, 2)
            act.sem_inc(z_free, 2)
            act.sem_inc(quad_free, 4)

            def used(tile):
                act.wait_ge(tile_used, tile + 3)

            act.wait_ge(consts_in, 48)
            ch.done(nc.scalar.activation(lam[:, 0, :], par[:, LL:LL + C], ACT.Abs))
            ch.wait()
            nc.scalar.activation(lam[:, 1, :], lam[:, 0, :], ACT.Exp, scale=-1.0).then_inc(lam_e, 1)
            act.wait_ge(var_ready, 1)
            nc.scalar.activation(sdev[:, :], veps[:, :], ACT.Sqrt).then_inc(sd_ready, 1)
            for u in range(2 * (TT + 1)):
                t, hh = u // 2, u % 2
                act.wait_ge(tr_done, u + 1)
                rows = META if t == 0 else P
                off = 0 if t == 0 else META + (t - 1) * P
                nc.scalar.activation(ht_hi[:, 4 * hh:4 * hh + 4, off:off + rows],
                                     ps[:, u % 8, :].rearrange("p (c t) -> p c t", c=4)[:, :, 0:rows],
                                     ACT.Copy).then_inc(ht_hi_done, 1)

            def x_out(n):
                used(n)
                src = ps[:, 2 * (n % 2):2 * (n % 2) + 2, 0:TH]
                if n < C:
                    if n >= 2:
                        act.wait_ge(conv_done, n - 1)
                    dst = xrp[:, n % 2, CONV - 1:].rearrange("p (h t) -> p h t", h=2)
                else:
                    dst = xp[:, n - C, :].rearrange("p (h t) -> p h t", h=2)
                nc.scalar.activation(dst, src, ACT.Copy).then_inc(x_evac, 1)

            def xc_high(c):
                act.wait_ge(conv_done, c + 1)
                if c >= 4:
                    act.wait_ge(gw_used, (c - 4) // 2 + 1)
                nc.scalar.activation(xc_hi[:, c % 4, :], xc[:, c % 4, :], ACT.Copy).then_inc(xc_hi_done, 1)

            def gates_out(n):
                for o in range(4):
                    k = 4 * n + o
                    act.wait_ge(ri_done, k + 1)
                    c = 2 * n + o % 2
                    dst = (R if o < 2 else I)[:, c, :].rearrange("p (h t) -> p h t", h=2)
                    bias = par[:, (BR if o < 2 else BI) + c:(BR if o < 2 else BI) + c + 1]
                    b = 4 + 2 * (k % 2)
                    nc.scalar.activation(dst, ps[:, b:b + 2, 0:TH], ACT.Sigmoid, bias=bias).then_inc(ri_evac, 1)

            x_out(0)
            x_out(1)
            xc_high(0)
            xc_high(1)
            for n in range(3):
                x_out(2 * n + 2)
                x_out(2 * n + 3)
                xc_high(2 * n + 2)
                xc_high(2 * n + 3)
                gates_out(n)
            x_out(8)
            x_out(9)
            gates_out(3)
            x_out(10)
            x_out(11)
            for g in range(POOL_GROUPS):
                act.wait_ge(pooled, g + 1)
                nc.scalar.activation(pl_hi[:, g, :], (psa, psb)[g % 2][:, META:T], ACT.Copy).then_inc(pl_hi_done, 1)
            for g in range(POOL_GROUPS):
                act.wait_ge(mix_done, g + 1)
                nc.scalar.activation(mixed_hi[:, g, :], ps[:, 4 + g, :], ACT.Identity,
                                     scale=par[:, PSC + g:PSC + g + 1]).then_inc(mixed_hi_done, 1)

            act.wait_ge(lam_ready, 1)
            act.wait_ge(gw_used, 4)
            act.wait_ge(mixed_split, POOL_C)
            for c in range(C):
                nc.scalar.activation(A[:, c, :], R[:, c, :], ACT.Exp, scale=lam[:, 8, c:c + 1]).then_inc(act_step, 1)
                ch.n += 1
                ch.wait()
                nc.scalar.activation(R[:, c, :], R[:, c, :], ACT.Tanh, scale=lam[:, 9, c:c + 1]).then_inc(at_done, 1)
            for c in range(C):
                act.wait_ge(m_done, c + 1)
                nc.scalar.activation(R[:, c, :], R[:, c, :], ACT.Sqrt).then_inc(mult_done, 1)

            def y_high(c):
                act.wait_ge(yf_done, c + 1)
                nc.scalar.activation(ya_hi[:, c, :], yf[:, c % 2, :], ACT.Copy).then_inc(ya_hi_done, 1)

            for c in range(C):
                used(T_GA + c)
                if c >= 2:
                    act.wait_ge(yf_done, c - 1)
                nc.scalar.activation(gel[:, c % 2, :], ps[:, c, :], ACT.Gelu_apprx_tanh).then_inc(gelu_done, 1)
                if c >= 1:
                    y_high(c - 1)
            y_high(C - 1)
            act.wait_ge(ya_split, C)
            with act.Fori(0, C) as i:
                for j in range(2):
                    act.wait_ge(tile_used, i * 2 + (T_GL + j + 3))
                    act.sem_inc(apart, 1)
                    nc.scalar.activation(gates[:, bass.ds(i * 2 + j, 1), :].rearrange("p a n -> p (a n)"),
                                         ps[:, j, :], ACT.Sigmoid).then_inc(gl_free, 1)
            with act.Fori(0, C // 2) as i:
                for j in range(2):
                    act.wait_ge(mf_done, i * 2 + (j + 1))
                    act.sem_inc(apart, 1)
                    nc.scalar.activation(mg_hi[:, bass.ds(i * 2 + j, 1), :].rearrange("p a n -> p (a n)"),
                                         m1[:, j, :], ACT.Copy).then_inc(mg_hi_done, 1)
            for t in range(TT):
                act.wait_ge(var_ready, 2 + t)
                nc.scalar.activation(sdev[:, t:t + 1], veps[:, t:t + 1], ACT.Sqrt).then_inc(sd_ready, 1)
            for t in range(TT):
                for hh in range(2):
                    u = 2 * t + hh
                    act.wait_ge(tr1_done, u + 1)
                    nc.scalar.activation(h1_hi[:, 4 * hh:4 * hh + 4, t * P:(t + 1) * P],
                                         ps[:, u, :].rearrange("p (c t) -> p c t", c=4), ACT.Copy)\
                        .then_inc(h1_hi_done, 1)
                nc.scalar.mul(htok[:, t, :], htok[:, t, :], ALPHA).then_inc(acc_ready, 1)

            with act.Fori(0, HEADS) as i:
                for j in range(2):
                    act.wait_ge(tile_used, i * 2 + (T_Q + j + 3))
                    act.wait_ge(s_done, i * 2 + (j + 1))
                    nc.scalar.activation(qf[:, j, :], ps[:, j, :], ACT.Copy).then_inc(q_free, 1)
                for j in range(2):
                    act.wait_ge(s_done, i * 2 + (j + 3))
                    act.sem_inc(apart, 1)
                    nc.scalar.activation(S_all[:, bass.ds(i * 2 + j, 1)].rearrange("p a t k -> p (a t k)"),
                                         ps[:, 2 + j, :], ACT.Copy).then_inc(s_free, 1)
            with act.Fori(0, GB * AHEAD // 2) as i:
                for j in range(2):
                    act.wait_ge(tile_used, i * 2 + (T_U + j + 3))
                    act.sem_inc(apart, 1)
                    nc.scalar.activation(G[:, bass.ds(i * 2 + j, 1), :].rearrange("p a n -> p (a n)"),
                                         ps[:, 4 + j, :], ACT.Gelu_apprx_tanh).then_inc(z_free, 1)

            def hidden_out(b, j, stored):
                act.wait_ge(tile_used, b + (T_US + 3))
                act.wait_ge(gst_stored[j % 2], stored)
                nc.scalar.activation(gst[:, j % 2, :], ps[:, 4 + j % 2, :], ACT.Gelu_apprx_tanh).then_inc(z_free, 1)

            with act.Fori(0, PRE // 2) as i:
                for j in range(2):
                    hidden_out(i * 2 + j, j, i * 16 + 16)
            act.wait_ge(cmax_ready, 1)
            nc.scalar.activation(cv_all[:, :, :, :], cv_all[:, :, :, :], ACT.Exp).then_inc(cexp_done, 1)
            for k in range(3):
                act.wait_ge(selT_done, k + 1)
                nc.scalar.activation(selT[:, k, :], ps[:, 6 + k if k < 2 else 0, :], ACT.Copy).then_inc(selT_ready, 1)
            with act.Fori(0, WCHUNKS // 2) as i:
                for s in range(2):
                    act.wait_ge(w_stored[s], i * 16 + 16)
                    for q in range(WT // 4):
                        act.wait_ge(quad_done, i * 16 + (s * 8 + q + 5))
                        nc.scalar.activation(wst[:, s, :, 4 * q:4 * q + 4],
                                             ps[:, q % 4, :].rearrange("p (t k) -> p k t", t=4), ACT.Copy)\
                            .then_inc(quad_free, 1)
                        if q % 4 == 3:
                            b = 2 * s + q // 4
                            hidden_out(i * BUILD + (PRE + b), b, i * 8 * BUILD + 16 * (PRE // 2 + 1 + b // 2))

            def v_high(k, dh):
                act.wait_ge(v_in[dh], k * 16 + 16)
                act.wait_ge(oe_done, k * 8 + (4 * dh + 12))
                nc.scalar.activation(vhi[:, dh], vraw[:, dh], ACT.Copy).then_inc(v_hi, 1)

            def a_high(k, slot, src):
                act.wait_ge(a_ready, k + 1)
                act.sem_inc(apart, 1)
                nc.scalar.activation(ahi[:, slot], src, ACT.Copy).then_inc(a_hi, 1)

            for b in range(SPILL - POST, SPILL):
                hidden_out(b, b, 16 * (b // 2 + 1))
                if b == SPILL - 6:
                    v_high(0, 0)
                    v_high(0, 1)
                if b == SPILL - 2:
                    a_high(0, 0, G[:, 0:GB, :])

            def next_group(k, slot, first_block):
                a_high(k, slot, G[:, first_block:first_block + GB, :])
                v_high(k, 0)
                v_high(k, 1)

            for k in range(1, AHEAD + 1):
                next_group(k, k % 2, k * GB if k < AHEAD else 0)
            with act.Fori(0, SPILLED // 2 - 1) as i:
                next_group(i * 2 + (AHEAD + 1), 1, GB)
                next_group(i * 2 + (AHEAD + 2), 0, 0)
            next_group(FIRST - 1, 1, GB)
            with act.Fori(0, (GROUPS - FIRST) // 2) as i:
                g = i * 2 + FIRST
                v_high(g, 0)
                v_high(g, 1)
                for b in range(2 * GB):
                    act.wait_ge(tile_used, i * 8 + (T_UD + b + 3))
                    if b % GB == 0:
                        act.wait_ge(a_split, i * 2 + (FIRST - 1 + b // GB))
                    nc.scalar.activation(G[:, b, :], ps[:, b % 2, :], ACT.Gelu_apprx_tanh).then_inc(z_free, 1)
                    if b == GB:
                        a_high(g, 0, G[:, 0:GB, :])
                a_high(g + 1, 1, G[:, GB:2 * GB, :])
                v_high(g + 1, 0)
                v_high(g + 1, 1)
            for t in range(TT):
                act.wait_ge(var_ready, 2 + TT + t)
                nc.scalar.activation(sdev[:, t:t + 1], veps[:, t:t + 1], ACT.Sqrt).then_inc(sd_ready, 1)

        @block.vector
        def _(dve):
            ch = Chain(dve, dve_step)
            dve.sem_inc(y_free, 2)
            dve.sem_inc(vraw_free[0], 1)
            dve.sem_inc(vraw_free[1], 1)
            dve.sem_inc(w_free[0], 1)
            dve.sem_inc(w_free[1], 1)
            dve.sem_inc(oe_free, 4)
            V = nc.vector

            def norm_stats(row, rows, k):
                for h in range(2):
                    ch.done(V.bn_stats(stats[0:rows, k, 6 * h:6 * h + 6], row[:, h * HD:(h + 1) * HD]))
                ch.wait()
                ch.done(V.bn_aggr(mv[0:rows, k, :], stats[0:rows, k, :]))

            def norm_apply(row, rows, k, bc, signal):
                ch.done(V.tensor_scalar(row, row, mv[0:rows, k, 0:1], rstd[0:rows, k:k + 1], ALU.subtract, ALU.mult))
                ch.wait()
                ch.done(V.tensor_tensor(row, row, bc[0:rows, 0, :], ALU.mult))
                ch.wait()
                V.tensor_tensor(row, row, bc[0:rows, 1, :], ALU.add).then_inc(signal, 1)

            ch.done(V.memset(mv[:, :, :], 1.0))
            ch.done(V.memset(xrp[:, :, 0:CONV - 1], 0.0))
            ch.wait()
            rows_of = [(hmeta[0:META, :], META)] + [(htok[:, t, :], P) for t in range(TT)]
            for k, (row, rows) in enumerate(rows_of):
                dve.wait_ge(x_in[k], 16)
                norm_stats(row, rows, k)
            ch.wait()
            V.tensor_scalar(veps[:, :], mv[:, :, 1], EPS, None, ALU.add).then_inc(var_ready, 1)
            dve.wait_ge(sd_ready, 1)
            ch.done(V.reciprocal(rstd[:, :], sdev[:, :]))
            ch.wait()
            dve.wait_ge(ln_in, 32)

            def ht_low(u):
                t, hh = u // 2, u % 2
                rows = META if t == 0 else P
                off = 0 if t == 0 else META + (t - 1) * P
                dve.wait_ge(ht_hi_done, u + 1)
                V.tensor_tensor(ht_lo[:, 4 * hh:4 * hh + 4, off:off + rows],
                                ps[:, u % 8, :].rearrange("p (c t) -> p c t", c=4)[:, :, 0:rows],
                                ht_hi[:, 4 * hh:4 * hh + 4, off:off + rows].bitcast(F32),
                                ALU.subtract).then_inc(ht_split, 1)

            for k, (row, rows) in enumerate(rows_of):
                norm_apply(row, rows, k, lnbc, h_ready)
                if k >= 1:
                    ht_low(2 * k - 2)
                    ht_low(2 * k - 1)
            ht_low(2 * TT)
            ht_low(2 * TT + 1)

            dve.wait_ge(lam_e, 1)
            e, s, z, q = lam[:, 1, :], lam[:, 3, :], lam[:, 4, :], lam[:, 5, :]
            ch.done(V.tensor_scalar(lam[:, 2, :], e, 2.0, None, ALU.add))
            ch.wait()
            ch.done(V.reciprocal(s, lam[:, 2, :]))
            ch.wait()
            ch.done(V.tensor_tensor(s, s, e, ALU.mult))
            ch.wait()
            ch.done(V.tensor_tensor(z, s, s, ALU.mult))
            ch.wait()
            ch.done(V.tensor_scalar(q, z, 1.0 / 17.0, None, ALU.mult))
            for k in (15, 13, 11, 9, 7, 5, 3):
                ch.wait()
                ch.done(V.scalar_tensor_tensor(q, q, 1.0 / k, z, ALU.add, ALU.mult))
            ch.wait()
            ch.done(V.scalar_tensor_tensor(q, q, 1.0, s, ALU.add, ALU.mult))
            ch.done(V.tensor_scalar(lam[:, 6, :], par[:, LL:LL + C], 0.0, LRU_C, ALU.min, ALU.mult))
            ch.wait()
            ch.done(V.scalar_tensor_tensor(lam[:, 8, :], q, -2.0 * LRU_C, lam[:, 6, :], ALU.mult, ALU.add))
            ch.wait()
            V.tensor_scalar(lam[:, 9, :], lam[:, 8, :], -1.0, None, ALU.mult).then_inc(lam_ready, 1)

            def conv(c):
                dve.wait_ge(x_evac, c + 1)
                if c >= 4:
                    ch.wait()
                    dve.wait_ge(xc_split, c - 3)
                x, y = xrp[:, c % 2, :], xc[:, c % 4, :]
                w = [par[:, CW + 4 * c + k:CW + 4 * c + k + 1] for k in range(CONV)]
                ch.done(V.tensor_scalar(y, x[:, CONV - 1:], w[CONV - 1], par[:, CB + c:CB + c + 1], ALU.mult, ALU.add))
                for k in range(CONV - 2, -1, -1):
                    ch.wait()
                    ins = V.scalar_tensor_tensor(y, x[:, k:k + T], w[k], y, ALU.mult, ALU.add)
                    if k:
                        ch.done(ins)
                    else:
                        ins.then_inc(conv_done, 1)

            def xc_low(c):
                dve.wait_ge(xc_hi_done, c + 1)
                V.tensor_tensor(xc_lo[:, c % 4, :], xc[:, c % 4, :], xc_hi[:, c % 4, :].bitcast(F32),
                                ALU.subtract).then_inc(xc_split, 1)

            def gated_input(n):
                dve.wait_ge(ri_evac, 4 * n + 4)
                for c in (2 * n, 2 * n + 1):
                    ch.done(V.tensor_tensor(I[:, c, :], I[:, c, :], xc[:, c % 4, :], ALU.mult))

            conv(0)
            conv(1)
            xc_low(0)
            xc_low(1)
            for n in range(3):
                conv(2 * n + 2)
                conv(2 * n + 3)
                xc_low(2 * n + 2)
                xc_low(2 * n + 3)
                gated_input(n)
            gated_input(3)

            for g in range(POOL_GROUPS):
                dve.wait_ge(x_evac, C + g + 1)
                if g >= 2:
                    dve.wait_ge(pl_hi_done, g - 1)
                if g >= 1:
                    dve.wait_ge(pl_hi_done, g)
                    V.tensor_tensor(pl_lo[:, g - 1, :], (psa, psb)[(g - 1) % 2][:, META:T],
                                    pl_hi[:, g - 1, :].bitcast(F32), ALU.subtract).then_inc(pl_split, 1)
                    dve.wait_ge(pl_split, g)
                levels = g + 1
                x0 = xp[:, g, :]
                src = x0
                for k in range(1, levels + 1):
                    start = META - ((1 << levels) - (1 << k))
                    sh = 1 << (k - 1)
                    dst = (psb, psa)[(g + levels - k) % 2]
                    ch.done(V.tensor_tensor(dst[:, start:T], src[:, start:T], src[:, start - sh:T - sh], ALU.add))
                    ch.wait()
                    src = dst
                out = (psa, psb)[g % 2]
                V.scalar_tensor_tensor(out[:, META:T], src[:, META:T], 1.0 / (1 << levels), x0[:, META:T],
                                       ALU.mult, ALU.subtract).then_inc(pooled, 1)
            g = POOL_GROUPS
            dve.wait_ge(pl_hi_done, g)
            V.tensor_tensor(pl_lo[:, g - 1, :], (psa, psb)[(g - 1) % 2][:, META:T],
                            pl_hi[:, g - 1, :].bitcast(F32), ALU.subtract).then_inc(pl_split, 1)
            for g in range(POOL_GROUPS):
                dve.wait_ge(mixed_hi_done, g + 1)
                V.scalar_tensor_tensor(mixed_lo[:, g, :], ps[:, 4 + g, :], par[:, PSC + g:PSC + g + 1],
                                       mixed_hi[:, g, :].bitcast(F32), ALU.mult, ALU.subtract).then_inc(mixed_split, 1)

            for c in range(C):
                dve.wait_ge(at_done, c + 1)
                if c >= 2:
                    dve.wait_ge(m_done, c - 1)
                tmp = (yf, gel)[c % 2].rearrange("p a n -> p (a n)")[:, 0:T]
                ch.done(V.tensor_tensor(tmp, A[:, c, :], A[:, c, :], ALU.mult))
                ch.wait()
                V.scalar_tensor_tensor(R[:, c, :], tmp, 1.0, R[:, c, :], ALU.add, ALU.mult).then_inc(m_done, 1)
            for c in range(C):
                dve.wait_ge(mult_done, c + 1)
                ch.done(V.tensor_tensor(I[:, c, :], I[:, c, :], R[:, c, :], ALU.mult))
                ch.wait()
                ch.done(V.tensor_tensor_scan(R[:, c, :], A[:, c, :], I[:, c, :], 0.0, ALU.mult, ALU.add))
            for c in range(C):
                dve.wait_ge(gelu_done, c + 1)
                ch.wait()
                if c >= 2:
                    dve.wait_ge(ya_split, c - 1)
                V.tensor_tensor(yf[:, c % 2, :], R[:, c, META:T], gel[:, c % 2, :], ALU.mult).then_inc(yf_done, 1)
                dve.wait_ge(ya_hi_done, c + 1)
                V.tensor_tensor(ya_lo[:, c, :], yf[:, c % 2, :], ya_hi[:, c, :].bitcast(F32),
                                ALU.subtract).then_inc(ya_split, 1)

            dve.wait_ge(gl_free, 2 + 2 * C)
            dve.wait_ge(ya_split, C)
            with dve.Fori(0, C // 2) as i:
                ch.enter(i, 6)
                for j in range(2):
                    m = i * 2 + j
                    dve.wait_ge(tile_used, i * 4 + (T_Y + 2 * j + 4))
                    dve.sem_inc(apart, 1)
                    for dst, off, bank in ((m1, 0, 2 + j), (m2, C, 4 + j)):
                        ch.done(V.tensor_tensor(dst[:, j, :],
                                                gates[:, bass.ds(m + off, 1), :].rearrange("p a n -> p (a n)"),
                                                ps[:, bank, :], ALU.mult))
                    ch.wait()
                    dve.sem_inc(y_free, 1)
                    V.tensor_tensor(m1[:, j, :], m1[:, j, :], m2[:, j, :], ALU.add).then_inc(mf_done, 1)
                    dve.wait_ge(mg_hi_done, i * 2 + (j + 1))
                    dve.sem_inc(apart, 1)
                    at_m = bass.ds(m, 1)
                    ch.done(V.tensor_tensor(mg_lo[:, at_m, :].rearrange("p a n -> p (a n)"), m1[:, j, :],
                                            mg_hi[:, at_m, :].rearrange("p a n -> p (a n)").bitcast(F32),
                                            ALU.subtract))
                    ch.wait()
                    dve.sem_inc(mg_split, 1)
                ch.leave(C // 2)

            dve.wait_ge(ln1_in, 32)
            for t in range(TT):
                dve.wait_ge(o_done, t + 1)
                for dh in range(2):
                    cols = slice(dh * HD, (dh + 1) * HD)
                    ch.done(V.scalar_tensor_tensor(htok[:, t, cols], htok[:, t, cols], ALPHA, ps[:, 2 * t + dh, :],
                                                   ALU.mult, ALU.add))
                ch.wait()
                norm_stats(htok[:, t, :], P, t)
                ch.wait()
                V.tensor_scalar(veps[:, t:t + 1], mv[:, t, 1:2], EPS, None, ALU.add).then_inc(var_ready, 1)
                dve.wait_ge(sd_ready, 2 + t)
                ch.done(V.reciprocal(rstd[:, t:t + 1], sdev[:, t:t + 1]))
                ch.wait()
                norm_apply(htok[:, t, :], P, t, lnbc, h1_ready)
            for u in range(2 * TT):
                t, hh = u // 2, u % 2
                dve.wait_ge(h1_hi_done, u + 1)
                V.tensor_tensor(h1_lo[:, 4 * hh:4 * hh + 4, t * P:(t + 1) * P],
                                ps[:, u, :].rearrange("p (c t) -> p c t", c=4),
                                h1_hi[:, 4 * hh:4 * hh + 4, t * P:(t + 1) * P].bitcast(F32),
                                ALU.subtract).then_inc(h1_split, 1)

            def top16(values, rest, v, ix, keep_apart):
                for t in range(TT):
                    ch.done(V.max(v(t, 0), values(t)))
                ch.wait()
                keep_apart()
                for t in range(TT):
                    ch.done(V.match_replace(out=rest(t), in_to_replace=v(t, 0), in_values=values(t), imm_value=NEG))
                for t in range(TT):
                    ch.done(V.max_index(ix(t, 0), v(t, 0), values(t)))
                ch.wait()
                keep_apart()
                for t in range(TT):
                    ch.done(V.max(v(t, 1), rest(t)))
                ch.wait()
                keep_apart()
                for t in range(TT):
                    ch.done(V.max_index(ix(t, 1), v(t, 1), rest(t)))

            def keep_apart():
                dve.sem_inc(apart, 1)

            with dve.Fori(0, HEADS) as i:
                ch.enter(i, 2 * 21 + 1 + 20 + 4)
                ch.wait()
                for j in range(2):
                    dve.wait_ge(s_free, i * 2 + (j + 3))
                    keep_apart()
                    ch.done(V.tensor_copy(S[:, :, :].rearrange("p t k -> p (t k)"),
                                          S_all[:, bass.ds(i * 2 + j, 1)].rearrange("p a t k -> p (a t k)")))
                    ch.wait()
                    keep_apart()
                    top16(lambda t: S[:, t, :], lambda t: S2[:, t, :],
                          lambda t, k: sv[:, j, t, 8 * k:8 * k + 8], lambda t, k: si[:, j, t, 8 * k:8 * k + 8],
                          keep_apart)
                    ch.wait()
                    keep_apart()
                a0 = sv[:, 0, :, :].unsqueeze(3).to_broadcast([P, TT, TOPK, TOPK])
                a1 = sv[:, 1, :, :].unsqueeze(2).to_broadcast([P, TT, TOPK, TOPK])
                ch.done(V.tensor_tensor(comb[:, :, :, :], a0, a1, ALU.add))
                ch.wait()
                keep_apart()
                flat = comb[:, :, :, :].rearrange("p t a b -> p t (a b)")
                top16(lambda t: flat[:, t, :], lambda t: comb2[:, t, :],
                      lambda t, k: cv[:, t, 8 * k:8 * k + 8], lambda t, k: ci[:, t, 8 * k:8 * k + 8], keep_apart)
                ch.wait()
                keep_apart()
                h = bass.ds(i, 1)
                ch.done(V.tensor_copy(cv_all[:, :, h, :].rearrange("p t a k -> p t (a k)"), cv[:, :, :]))
                ch.done(V.tensor_copy(ci_all[:, :, h, :].rearrange("p t a k -> p t (a k)"), ci[:, :, :]))
                for j in range(2):
                    ch.done(V.tensor_copy(si_all[:, j, :, h, :].rearrange("p t a k -> p t (a k)"), si[:, j, :, :]))
                ch.leave(HEADS)
            ch.wait()
            flat_cv = cv_all[:, :, :, :].rearrange("p t h k -> p (t h) k")
            ch.done(V.tensor_copy(ssum[:, 0, :].unsqueeze(2), flat_cv[:, :, 0:1]))
            ch.wait()
            V.tensor_tensor(flat_cv, flat_cv, ssum[:, 0, :].unsqueeze(2).to_broadcast([P, TT * HEADS, TOPK]),
                            ALU.subtract).then_inc(cmax_ready, 1)
            flat_ci = ci_all[:, :, :, :].rearrange("p t h k -> p (t h k)")
            ch.done(V.tensor_scalar(cdiv[:, 0, :], flat_ci, 4, None, ALU.logical_shift_right))
            ch.done(V.tensor_scalar(cdiv[:, 1, :], flat_ci, TOPK - 1, None, ALU.bitwise_and))
            ch.wait()
            ch.done(V.tensor_copy(cidx[:, :, :], cdiv[:, :, :]))
            ch.wait()
            for k in range(2):
                keys_of = si_all[:, k].rearrange("p t h k -> p (t h) k")
                for j in range(TOPK):
                    ch.done(V.scalar_tensor_tensor(
                        prod[:, j, :].rearrange("p (a k) -> p a k", k=TOPK),
                        cidx[:, k, :].rearrange("p (a k) -> p a k", k=TOPK), float(j),
                        keys_of[:, :, j:j + 1].to_broadcast([P, TT * HEADS, TOPK]), ALU.is_equal, ALU.mult))
                ch.wait()
                ch.done(V.tensor_reduce(sel[:, k, :], prod[:, :, :].rearrange("p j s -> p s j"), AX_X, ALU.add))
                ch.wait()
            dve.wait_ge(cexp_done, 1)
            ch.done(V.tensor_reduce(ssum[:, 0, :], flat_cv, AX_X, ALU.add))
            ch.wait()
            ch.done(V.reciprocal(ssum[:, 1, :], ssum[:, 0, :]))
            ch.wait()
            V.tensor_tensor(sel[:, 2, :].rearrange("p (a k) -> p a k", k=TOPK), flat_cv,
                            ssum[:, 1, :].unsqueeze(2).to_broadcast([P, TT * HEADS, TOPK]),
                            ALU.mult).then_inc(sel_ready, 1)

            dve.wait_ge(selT_ready, 3)
            dve.sem_inc(oh_ready, 1)
            with dve.Fori(0, WCHUNKS // 2) as i:
                ch.enter(i, 3)
                dve.wait_ge(oh_ready, i * 16 + 1)
                keep_apart()
                for k in range(3):
                    ch.done(V.tensor_copy(cur[:, k, :], selT[:, k, bass.ds(i * 64, 64)]))
                ch.wait()
                for q in range(16):
                    dve.wait_ge(quad_done, i * 16 + (q + 1))
                    keep_apart()
                    for t in range(4):
                        e, tok = 4 * (q % 4) + t, 4 * q + t
                        V.tensor_scalar(oh2[:, e, :], iota[:, :], cur[:, 1, tok:tok + 1], None, ALU.is_equal)
                        ins = V.tensor_scalar(oh1[:, e, :], iota[:, :], cur[:, 0, tok:tok + 1],
                                              cur[:, 2, tok:tok + 1], ALU.is_equal, ALU.mult)
                    ins.then_inc(oh_ready, 1)
                ch.leave(WCHUNKS // 2)

            def v_low(k, dh):
                dve.wait_ge(v_hi, k * 2 + (dh + 1))
                V.tensor_tensor(vlo[:, dh], vraw[:, dh], vhi[:, dh].bitcast(F32), ALU.subtract).then_inc(v_split, 1)
                dve.wait_ge(v_split, k * 2 + (dh + 1))
                dve.sem_inc(vraw_free[dh], 1)

            def weigh(k, slot, i, blocks, spilled):
                dve.wait_ge(w_in[slot], i * 16 + 16)
                dve.wait_ge(z_free, k * GB + (GB + 2))
                if spilled is not None:
                    dve.wait_ge(g_in[slot], spilled * 16 + 16)
                dve.wait_ge(oe_done, k * 8 + 8)
                V.tensor_tensor(blocks.rearrange("p b (c t) -> p b c t", t=WT),
                                blocks.rearrange("p b (c t) -> p b c t", t=WT),
                                wt[:, slot].rearrange("p c b t -> p b c t"), ALU.mult).then_inc(a_ready, 1)
                dve.wait_ge(a_ready, k + 1)
                dve.sem_inc(w_free[slot], 1)

            def a_low(k, slot, blocks):
                dve.wait_ge(a_hi, k + 1)
                V.tensor_tensor(alo[:, slot], blocks, ahi[:, slot].bitcast(F32), ALU.subtract).then_inc(a_split, 1)

            def sum_up(k, dh, t):
                dve.wait_ge(oe_done, k * 8 + (dh * 4 + t + 17))
                dve.wait_ge(oe_free, k * 8 + (dh * 4 + t + 1))
                cols = slice(dh * HD, (dh + 1) * HD)
                V.tensor_tensor(htok[:, t, cols], htok[:, t, cols], ps[:, 4 + t, :], ALU.add).then_inc(oe_free, 1)

            def sums(k, dh):
                for t in range(TT):
                    sum_up(k, dh, t)

            def step(k, nxt=None):
                if nxt is not None:
                    n, slot, use, first_block, spilled = nxt
                    blocks = G[:, first_block:first_block + GB, :]
                    weigh(n, slot, use, blocks, spilled)
                    a_low(n, slot, blocks)
                for dh in range(2):
                    sums(k, dh)
                    if nxt is not None:
                        v_low(n, dh)

            dve.wait_ge(acc_ready, TT)
            dve.wait_ge(w_stored[0], 16 * (WCHUNKS // 2 + 1))
            dve.wait_ge(w_stored[1], 16 * (WCHUNKS // 2 + 1))
            v_low(0, 0)
            v_low(0, 1)
            weigh(0, 0, 0, G[:, 0:GB, :], None)
            a_low(0, 0, G[:, 0:GB, :])
            for k in range(1, AHEAD + 1):
                step(k - 1, (k, k % 2, k // 2, k * GB if k < AHEAD else 0, None if k < AHEAD else 0))
            with dve.Fori(0, SPILLED // 2 - 1) as i:
                step(i * 2 + AHEAD, (i * 2 + (AHEAD + 1), 1, i + AHEAD // 2, GB, i))
                step(i * 2 + (AHEAD + 1), (i * 2 + (AHEAD + 2), 0, i + (AHEAD // 2 + 1), 0, i + 1))
            step(FIRST - 2, (FIRST - 1, 1, FIRST // 2 - 1, GB, SPILLED // 2 - 1))
            step(FIRST - 1)
            with dve.Fori(0, (GROUPS - FIRST) // 2) as i:
                k = i * 2 + FIRST
                v_low(k, 0)
                v_low(k, 1)
                for s in range(2):
                    blocks = G[:, s * GB:(s + 1) * GB, :]
                    weigh(k + s, s, i + FIRST // 2, blocks, None)
                    a_low(k + s, s, blocks)
                sums(k, 0)
                v_low(k + 1, 0)
                sums(k, 1)
                v_low(k + 1, 1)
                sums(k + 1, 0)
                sums(k + 1, 1)

            dve.wait_ge(ln2_in, 32)
            dve.wait_ge(oe_free, 4 + GROUPS * 8)
            for t in range(TT):
                norm_stats(htok[:, t, :], P, t)
                ch.wait()
                V.tensor_scalar(veps[:, t:t + 1], mv[:, t, 1:2], EPS, None, ALU.add).then_inc(var_ready, 1)
            for t in range(TT):
                dve.wait_ge(sd_ready, 2 + TT + t)
                ch.done(V.reciprocal(rstd[:, t:t + 1], sdev[:, t:t + 1]))
                ch.wait()
                norm_apply(htok[:, t, :], P, t, ln2bc, out_ready)


def kernel(x, meta, ln_in_g, ln_in_b, w_in, conv_w, conv_b, w_rg, b_rg, w_ig, b_ig, lru_L,
           w_proj_a, pool_w, pool_scale, w_proj_b, w_out, ln1_g, ln1_b, w_q, sub_keys,
           expert_u, expert_v, ln2_g, ln2_b):
    import numpy as np
    import concourse.bacc as bacc
    from concourse.bass_utils import run_bass_kernel_spmd

    nc = bacc.Bacc("TRN2", target_bir_lowering=False, num_devices=1)
    arrays, args = {}, []

    def give(name, a):
        a = np.ascontiguousarray(a)
        arrays[name] = a
        args.append(nc.dram_tensor(name, a.shape, mybir.dt.from_np(a.dtype), kind="ExternalInput").ap())

    def columns(v):
        return np.asarray(v).reshape(-1, P).T

    def stationary(w):
        w = np.asarray(w)
        k, n = w.shape
        return w.reshape(k // P, P, n // P, P).transpose(2, 1, 0, 3).reshape(n // P, P, k)

    w = np.asarray(w_in)[0]
    n_pool = POOL_C * P
    give("x_d", np.asarray(x).reshape(TT, P, D))
    give("meta_d", meta)
    give("ln_d", np.stack([np.asarray(v).reshape(-1) for v in (ln_in_g, ln_in_b, ln1_g, ln1_b, ln2_g, ln2_b)]))
    cw = np.asarray(conv_w)[0].reshape(CONV, C, P).transpose(2, 1, 0).reshape(P, C * CONV)
    give("par_d", np.concatenate([cw, columns(conv_b), columns(b_rg), columns(b_ig), columns(lru_L),
                                  columns(pool_scale)], axis=1))
    give("ident_d", np.eye(P, dtype=np.float32))
    give("iota_d", np.tile(np.arange(P, dtype=np.float32), (P, 1)))
    give("wxr_d", stationary(w[:, 0:D]))
    give("wxp_d", stationary(w[:, 2 * D:2 * D + n_pool]))
    give("wga_d", stationary(w[:, D:2 * D]))
    give("wgl_d", stationary(w[:, 2 * D + n_pool:]))
    gw = np.stack([np.asarray(w_rg)[0], np.asarray(w_ig)[0]], axis=1)
    give("wrgig_d", gw.reshape(4, 2, 2, P, 256).transpose(0, 3, 1, 2, 4).reshape(4, P, D))
    give("poolw_d", np.asarray(pool_w)[0].transpose(1, 0, 2).reshape(P, POOL_GROUPS * P))
    give("wpa_d", stationary(np.asarray(w_proj_a)[0]))
    give("wpb_d", stationary(np.asarray(w_proj_b)[0]))
    give("wo_d", np.asarray(w_out)[0].reshape(C, P, D))
    give("wq_d", stationary(np.asarray(w_q)[0]))
    give("keys_d", np.asarray(sub_keys)[0].reshape(2 * HEADS, KEYS, P).transpose(2, 0, 1))
    give("u_d", np.asarray(expert_u)[0].reshape(KEYS, P, C, P).transpose(0, 3, 2, 1).reshape(KEYS, P, D))
    give("v_d", np.asarray(expert_v)[0].reshape(GROUPS, GB, P, 2, HD).transpose(0, 3, 2, 1, 4)
         .reshape(2 * GROUPS, P, GB * HD))
    out = nc.dram_tensor("out_d", (TT, P, D), F32, kind="ExternalOutput")
    layer(nc, *args, out.ap())
    r = run_bass_kernel_spmd(nc, [arrays], core_ids=[0])
    return r.results[0]["out_d"].reshape(1, N, D)
```

```python
from contextlib import ExitStack

import concourse.bass as bass
from concourse import mybir

F32 = mybir.dt.float32
F32R = mybir.dt.float32r
BF16 = mybir.dt.bfloat16
U32 = mybir.dt.uint32
ALU = mybir.AluOpType
ACT = mybir.ActivationFunctionType
AX_X = mybir.AxisListType.X

P = 128
D = 1024
META = 16
N = 512
T = META + N
TH = T // 2
C = D // P
TT = N // P
HD = D // 2
POOL_GROUPS = 4
POOL_C = POOL_GROUPS
CONV = 4
HEADS = 8
KEYS = 128
TOPK = 16
SEL = HEADS * TOPK
ALPHA = 2.0 ** 0.25
EPS = 1e-5
LRU_C = 8.0
GB = 4
GROUPS = KEYS // GB
AHEAD = 4
PRE, MID, BUILD, POST = 12, 4, 4, 8
EXP_AHEAD = 4
WT = 32
OCT = 8
WCHUNKS = N // WT
SPILL = PRE + MID + BUILD * WCHUNKS // 2 + POST
SPILLED = SPILL // GB
FIRST = AHEAD + SPILLED
NEG = -3.0e38

CW, CB, BR, BI, LL, PSC = 0, 32, 40, 48, 56, 64
NPAR = 68


class Chain:

    def __init__(self, eng, sem):
        self.eng, self.sem, self.base, self.n, self.off = eng, sem, 0, 0, None

    def done(self, ins):
        ins.then_inc(self.sem, 1)
        self.n += 1

    def value(self):
        return self.base + self.n if self.off is None else self.off + self.n

    def wait(self):
        self.eng.wait_ge(self.sem, self.value())

    def enter(self, i, per):
        self.base, self.n, self.per = self.base + self.n, 0, per
        self.off = i * per + self.base

    def leave(self, times):
        assert self.n == self.per, (self.n, self.per)
        self.base, self.n, self.off = self.base + times * self.per, 0, None


def layer(nc, x_d, meta_d, ln_d, par_d, ident_d, iota_d, wxr_d, wxp_d, wga_d, wgl_d, wrgig_d, poolw_d,
          wpa_d, wpb_d, wo_d, wq_d, keys_d, u_d, v_d, out_d):
    w_spill = nc.dram_tensor("w_spill", [WCHUNKS, P, KEYS, WT], F32).ap()
    g_spill = nc.dram_tensor("g_spill", [SPILL, P, N], F32).ap()

    base = (nc.sbuf_base + 63) // 64 * 64
    top = [base]

    def at(name, shape, dt, offset):
        return nc.alloc_sbuf_tensor_at(name, shape, dt, offset=offset)

    def size(shape):
        n = 4
        for s in shape[1:]:
            n *= s
        return n

    def place(name, shape, dt, cursor):
        t = at(name, shape, dt, cursor[0])
        cursor[0] += (size(shape) // (2 if dt == BF16 else 1) + 31) // 32 * 32
        assert cursor[0] <= nc.sbuf_usable_end, (name, cursor[0] - nc.sbuf_usable_end)
        return t

    wraw = place("wraw", [P, 2, D], F32, top)
    whi = place("whi", [P, 2, D], F32R, top)
    wlo = place("wlo", [P, 2, D], F32R, top)
    htok = place("htok", [P, TT, D], F32, top)
    ident = place("ident", [P, P], F32, top)
    iota = place("iota", [P, P], F32, top)
    par = place("par", [P, NPAR], F32, top)
    lam = place("lam", [P, 10, C], F32, top)
    stats = place("stats", [P, 5, 12], F32, top)
    mv = place("mv", [P, 5, 2], F32, top)
    veps = place("veps", [P, 5], F32, top)
    sdev = place("sdev", [P, 5], F32, top)
    rstd = place("rstd", [P, 5], F32, top)
    seq = top[0]
    ht_hi = place("ht_hi", [P, C, T], F32R, top)
    ht_lo = place("ht_lo", [P, C, T], F32R, top)
    h1_hi = at("h1_hi", [P, C, N], F32R, seq)
    h1_lo = at("h1_lo", [P, C, N], F32R, seq + size([P, C, N]))
    lnbc_at = nc.sbuf_usable_end // 64 * 64 - 2 * D * 4
    lnbc = at("lnbc", [P, 2, D], F32, lnbc_at)

    region = top[0]
    r = [region]
    R = place("R", [P, C, T], F32, r)
    I = place("I", [P, C, T], F32, r)
    mixed_hi = place("mixed_hi", [P, POOL_C, N], F32R, r)
    mixed_lo = place("mixed_lo", [P, POOL_C, N], F32R, r)
    after_mixed = r[0]
    xrp = place("xrp", [P, 2, CONV - 1 + T], F32, r)
    xc = place("xc", [P, 4, T], F32, r)
    xc_hi = place("xc_hi", [P, 4, T], F32R, r)
    xc_lo = place("xc_lo", [P, 4, T], F32R, r)
    gwraw = place("gwraw", [P, D], F32, r)
    gwhi = place("gwhi", [P, D], F32R, r)
    gwlo = place("gwlo", [P, D], F32R, r)
    xp = place("xp", [P, POOL_C, T], F32, r)
    psa = place("psa", [P, T], F32, r)
    psb = place("psb", [P, T], F32, r)
    pl_hi = place("pl_hi", [P, POOL_C, N], F32R, r)
    hmeta = at("hmeta", [P, D], F32, r[0])
    pl_lo = place("pl_lo", [P, POOL_C, N], F32R, r)
    assert r[0] <= lnbc_at, r[0] - lnbc_at
    r = [after_mixed]
    ya_hi = place("ya_hi", [P, C, N], F32R, r)
    ya_lo = place("ya_lo", [P, C, N], F32R, r)
    after_ya = r[0]
    A = place("A", [P, C, T], F32, r)
    gel = place("gel", [P, 2, N], F32, r)
    yf = place("yf", [P, 2, N], F32, r)
    assert r[0] <= lnbc_at
    r = [region]
    r_g = [after_ya]
    gates = place("gates", [P, 2 * C, N], F32, r_g)
    m1 = place("m1", [P, 2, N], F32, r_g)
    m2 = place("m2", [P, 2, N], F32, r_g)
    assert r_g[0] <= lnbc_at, r_g[0] - lnbc_at
    mg_hi = at("mg_hi", [P, C, N], F32R, region)
    mg_lo = at("mg_lo", [P, C, N], F32R, region + size([P, C, N]))
    assert region + 2 * size([P, C, N]) <= region + 2 * size([P, C, T])
    wo_hi, wo_lo = [], []
    for half, start in enumerate((seq, region + 2 * size([P, C, T]))):
        wo_hi.append(at(f"wo_hi{half}", [P, C // 2, D], F32R, start))
        wo_lo.append(at(f"wo_lo{half}", [P, C // 2, D], F32R, start + size([P, C // 2, D])))
    assert seq + 2 * size([P, C // 2, D]) <= region
    assert region + 2 * size([P, C, T]) + 2 * size([P, C // 2, D]) <= after_ya
    r = [region]
    G = place("G", [P, GB * AHEAD, N], F32, r)
    after_g = r[0]
    keys = place("keys", [P, 2 * HEADS, KEYS], F32, r)
    qf = place("qf", [P, 2, N], F32, r)
    S = place("S", [P, TT, KEYS], F32, r)
    S2 = place("S2", [P, TT, KEYS], F32, r)
    sv = place("sv", [P, 2, TT, TOPK], F32, r)
    si = place("si", [P, 2, TT, TOPK], U32, r)
    comb = place("comb", [P, TT, TOPK, TOPK], F32, r)
    comb2 = place("comb2", [P, TT, TOPK * TOPK], F32, r)
    cv = place("cv", [P, TT, TOPK], F32, r)
    ci = place("ci", [P, TT, TOPK], U32, r)
    cv_all = place("cv_all", [P, TT, HEADS, TOPK], F32, r)
    ci_all = place("ci_all", [P, TT, HEADS, TOPK], U32, r)
    si_all = place("si_all", [P, 2, TT, HEADS, TOPK], F32, r)
    cdiv = place("cdiv", [P, 2, TT * SEL], U32, r)
    cidx = place("cidx", [P, 2, TT * SEL], F32, r)
    sel = place("sel", [P, 3, TT * SEL], F32, r)
    ssum = place("ssum", [P, 2, TT * HEADS], F32, r)
    selT_at = r[0] = max(r[0], after_g + size([P, 2, GB, N]) + 2 * size([P, 2, GB, HD]))
    selT = place("selT", [P, 3, N], F32, r)
    cur = place("cur", [P, 2, OCT], BF16, r)
    wrest = place("wrest", [P, N], F32, r)
    wparts = place("wparts", [P, 3, N], BF16, r)
    iota4 = place("iota4", [P, KEYS, 4], BF16, r)
    r_oh = [after_g]
    oh2 = place("oh2", [P, 2, 2, KEYS, 4], BF16, r_oh)
    ohw = place("ohw", [P, 2, 3, 2, KEYS, 4], BF16, r_oh)
    oh1 = place("oh1", [P, 2, KEYS, 4], BF16, r)
    wst_at = r[0]
    wst = place("wst", [P, 2, KEYS, WT], F32, r)
    S_all = at("S_all", [P, 2 * HEADS, TT, KEYS], F32, wst_at)
    prod = at("prod", [P, TOPK, TT * SEL], F32, wst_at)
    r2 = [after_g]
    alo = place("alo", [P, 2, GB, N], F32R, r2)
    vraw_at = r2[0]
    vraw = place("vraw", [P, 2, GB, HD], F32, r2)
    vhi = place("vhi", [P, 2, GB, HD], F32R, r2)
    assert r2[0] <= selT_at
    vlo = place("vlo", [P, 2, GB, HD], F32R, r2)
    wt = place("wt", [P, 2, WCHUNKS, GB, WT], F32, r2)
    ahi = place("ahi", [P, 2, GB, N], F32R, r2)
    assert r_oh[0] <= vraw_at
    gst = place("gst", [P, 2, N], F32, [max(r[0], r2[0])])
    ln2bc = at("ln2bc", [P, 2, D], F32, vraw_at)

    ctx = ExitStack()
    with ctx:
        ps = ctx.enter_context(nc.psum_tensor("ps", [P, 8, 512], F32))

        def sem(name):
            return ctx.enter_context(nc.semaphore(name))

        consts_in = sem("consts_in")
        ln_in = sem("ln_in")
        ln1_in = sem("ln1_in")
        ln2_in = sem("ln2_in")
        x_in = [sem(f"x_in{t}") for t in range(TT + 1)]
        raw_in = [sem("raw_in0"), sem("raw_in1")]
        raw_free = sem("raw_free")
        tile_hi = sem("tile_hi")
        tile_split = sem("tile_split")
        tile_used = sem("tile_used")
        gw_in = sem("gw_in")
        gw_free = sem("gw_free")
        gw_split = sem("gw_split")
        gw_used = sem("gw_used")
        wo_split = sem("wo_split")
        dve_step = sem("dve_step")
        act_step = sem("act_step")
        apart = sem("apart")
        var_ready = sem("var_ready")
        sd_ready = sem("sd_ready")
        h_ready = sem("h_ready")
        tr_done = sem("tr_done")
        ht_hi_done = sem("ht_hi_done")
        ht_split = sem("ht_split")
        lam_e = sem("lam_e")
        lam_ready = sem("lam_ready")
        x_evac = sem("x_evac")
        conv_done = sem("conv_done")
        xc_hi_done = sem("xc_hi_done")
        xc_split = sem("xc_split")
        ri_done = sem("ri_done")
        ri_evac = sem("ri_evac")
        pooled = sem("pooled")
        pl_hi_done = sem("pl_hi_done")
        pl_split = sem("pl_split")
        mix_done = sem("mix_done")
        mixed_hi_done = sem("mixed_hi_done")
        mixed_split = sem("mixed_split")
        at_done = sem("at_done")
        m_done = sem("m_done")
        mult_done = sem("mult_done")
        gelu_done = sem("gelu_done")
        yf_done = sem("yf_done")
        ya_hi_done = sem("ya_hi_done")
        ya_split = sem("ya_split")
        gl_free = sem("gl_free")
        y_free = sem("y_free")
        mf_done = sem("mf_done")
        mg_hi_done = sem("mg_hi_done")
        mg_split = sem("mg_split")
        o_done = sem("o_done")
        h1_ready = sem("h1_ready")
        tr1_done = sem("tr1_done")
        h1_hi_done = sem("h1_hi_done")
        h1_split = sem("h1_split")
        acc_ready = sem("acc_ready")
        keys_in = sem("keys_in")
        q_free = sem("q_free")
        s_done = sem("s_done")
        s_free = sem("s_free")
        z_free = sem("z_free")
        cmax_ready = sem("cmax_ready")
        cexp_done = sem("cexp_done")
        sel_ready = sem("sel_ready")
        selT_done = sem("selT_done")
        selT_ready = sem("selT_ready")
        oh_part = sem("oh_part")
        oh_ready = sem("oh_ready")
        quad_done = sem("quad_done")
        quad_free = sem("quad_free")
        gst_stored = [sem("gst_stored0"), sem("gst_stored1")]
        g_in = [sem("g_in0"), sem("g_in1")]
        w_stored = [sem("w_stored0"), sem("w_stored1")]
        v_in = [sem("v_in0"), sem("v_in1")]
        vraw_free = [sem("vraw_free0"), sem("vraw_free1")]
        v_hi = sem("v_hi")
        v_split = sem("v_split")
        w_in = [sem("w_in0"), sem("w_in1")]
        w_free = [sem("w_free0"), sem("w_free1")]
        a_ready = sem("a_ready")
        a_hi = sem("a_hi")
        a_split = sem("a_split")
        oe_done = sem("oe_done")
        oe_free = sem("oe_free")
        out_ready = sem("out_ready")
        out_stored = sem("out_stored")

        T_XR, T_XP, T_GA = 0, C, C + POOL_C
        T_GL = T_GA + C
        T_Y = T_GL + 2 * C
        T_Q = T_Y + C + C // 2
        T_U = T_Q + 2 * HEADS
        T_US = T_U + GB * AHEAD
        T_UD = T_U + GB * FIRST
        T_END = T_U + KEYS
        TR_BANK = (0, 1, 2, 3, 4, 5, 6, 7, 4, 5)
        A_BANK, B_BANK = (2, 3, 0, 1), (4, 5, 6, 7)
        RAW_WO = C

        BY_HALF = [(dh, t) for dh in range(2) for t in range(TT)]
        BY_TILES = [(0, 0), (0, 1), (1, 0), (1, 1), (0, 2), (1, 2), (0, 3), (1, 3)]

        IN_PARTS = (slice(0, 3), slice(3, TT + 1))
        SD = len(IN_PARTS)

        block = ctx.enter_context(nc.Block())

        @block.sync
        def _(sp):
            def load(n, src, cols=D):
                tile, slot = n
                sp.wait_ge(raw_free, tile + 1)
                sp.dma_start(wraw[:, slot, 0:cols], src).then_inc(raw_in[slot], 16)

            def one(d, k):
                return d[bass.ds(k, 1)].rearrange("a p n -> (a p) n")

            def x_load(t):
                sp.dma_start(htok[:, t, :], x_d[t]).then_inc(x_in[t + 1], 16)

            sp.dma_start(hmeta[0:META, :], meta_d).then_inc(x_in[0], 16)
            x_load(0)
            x_load(1)
            for k in range(2):
                sp.dma_start(lnbc[:, k, :], ln_d[k:k + 1, :].partition_broadcast(P)).then_inc(ln_in, 16)
            x_load(2)
            x_load(3)
            sp.dma_start(ident[:, :], ident_d).then_inc(consts_in, 16)
            sp.dma_start(iota[:, :], iota_d).then_inc(consts_in, 16)
            sp.dma_start(par[:, :], par_d).then_inc(consts_in, 16)

            def gate_weights(k):
                sp.wait_ge(gw_free, k + 1)
                if k < 4:
                    sp.dma_start(gwraw[:, :], wrgig_d[k]).then_inc(gw_in, 16)
                else:
                    sp.dma_start(gwraw[:, 0:N], poolw_d).then_inc(gw_in, 16)

            for c in range(C):
                load((T_XR + c, c % 2), wxr_d[c])
                if c % 2 == 1:
                    gate_weights(c // 2)
            for c in range(POOL_C):
                load((T_XP + c, c % 2), wxp_d[c])
            gate_weights(4)
            for c in range(C):
                load((T_GA + c, c % 2), wga_d[c])
            with sp.Fori(0, C) as i:
                for j in range(2):
                    load((i * 2 + (T_GL + j), j), one(wgl_d, i * 2 + j))
            with sp.Fori(0, C // 4) as i:
                for j in range(2):
                    for k, src in enumerate((one(wpa_d, i * 4 + 2 * j), one(wpa_d, i * 4 + (2 * j + 1)),
                                             one(wpb_d, i * 2 + j))):
                        load((i * 6 + (T_Y + 3 * j + k), (j + k) % 2), src)
            sp.wait_ge(ht_split, 2 * (TT + 1))
            for k in range(2):
                sp.dma_start(lnbc[:, k, :], ln_d[2 + k:3 + k, :].partition_broadcast(P)).then_inc(ln1_in, 16)
            for c in range(C):
                load((T_Q + c, c % 2), wo_d[c])
            for j in range(2):
                load((T_Q + RAW_WO + j, j), wq_d[j])
            sp.wait_ge(o_done, TT)
            sp.dma_start(keys[:, :, :], keys_d).then_inc(keys_in, 16)
            with sp.Fori(1, HEADS) as i:
                for j in range(2):
                    load((i * 2 + (T_Q + RAW_WO + j), j), one(wq_d, i * 2 + j))
            with sp.Fori(0, GB * AHEAD // 2) as i:
                for j in range(2):
                    load((i * 2 + (T_U + RAW_WO + j), j), one(u_d, i * 2 + j))
            def u_load(b, j):
                load((b + (T_US + RAW_WO), j % 2), one(u_d, b + GB * AHEAD))

            def g_store(b, j):
                sp.wait_ge(z_free, b + (GB * AHEAD + 3))
                sp.dma_start(g_spill[bass.ds(b, 1)].rearrange("a p n -> (a p) n"), gst[:, j % 2, :])\
                    .then_inc(gst_stored[j % 2], 16)

            LOOK = 3
            sp.sem_inc(gst_stored[0], 16)
            sp.sem_inc(gst_stored[1], 16)
            for b in range(LOOK):
                u_load(b, b)
            with sp.Fori(0, (PRE + MID) // 2) as i:
                for j in range(2):
                    u_load(i * 2 + (j + LOOK), j + LOOK)
                    g_store(i * 2 + j, j)
            sp.sem_inc(w_stored[0], 16)
            sp.sem_inc(w_stored[1], 16)
            with sp.Fori(0, WCHUNKS // 2) as i:
                for s in range(2):
                    for j in range(2):
                        b = 2 * s + j
                        u_load(i * BUILD + (PRE + MID + b + LOOK), b + LOOK)
                        if j == 1:
                            sp.wait_ge(quad_free, i * 16 + (4 + 8 * (s + 1)))
                            sp.dma_start(w_spill[bass.ds(i * 2 + s, 1)].rearrange("a p k t -> (a p) (k t)"),
                                         wst[:, s].rearrange("p k t -> p (k t)")).then_inc(w_stored[s], 16)
                        g_store(i * BUILD + (PRE + MID + b), b)

            def v_load(g, k, dh):
                sp.wait_ge(vraw_free[dh], k + 1)
                sp.dma_start(vraw[:, dh].rearrange("p b n -> p (b n)"),
                             v_d[bass.ds(g * 2 + dh, 1)].rearrange("a p n -> (a p) n")).then_inc(v_in[dh], 16)

            def w_load(g, slot, k):
                sp.wait_ge(w_free[slot], k + 1)
                sp.dma_start(wt[:, slot].rearrange("p c k t -> p c (k t)"),
                             w_spill[:, :, bass.ds(g * GB, GB), :].rearrange("c p k t -> p c (k t)"))\
                    .then_inc(w_in[slot], 16)

            for b in range(POST):
                if b + LOOK < POST:
                    u_load(SPILL - POST + b + LOOK, b + LOOK)
                g_store(SPILL - POST + b, b)
                if b < 2:
                    v_load(0, 0, b)
                if b == 2:
                    sp.wait_ge(w_stored[0], 16 * (WCHUNKS // 2 + 1))
                    sp.wait_ge(w_stored[1], 16 * (WCHUNKS // 2 + 1))
                    w_load(0, 0, 0)
                if b == 4:
                    w_load(1, 1, 0)
            for j in range(2):
                sp.wait_ge(gst_stored[j], 16 * (SPILL // 2 + 1))

            def g_load(g, slot):
                sp.wait_ge(a_split, g - 1)
                sp.dma_start(G[:, slot * GB:(slot + 1) * GB, :],
                             g_spill[bass.ds((g - AHEAD) * GB, GB)].rearrange("b p n -> p b n"))\
                    .then_inc(g_in[slot], 16)

            for g in range(1, AHEAD):
                w_load(g + 1, (g + 1) % 2, (g + 1) // 2)
                if g + 1 == AHEAD:
                    g_load(g + 1, (g + 1) % 2)
                v_load(g, g, 0)
                v_load(g, g, 1)
            with sp.Fori(0, SPILLED // 2 - 1) as i:
                for s in range(2):
                    g = i * 2 + (AHEAD + s)
                    w_load(i * 2 + (AHEAD + s + 1), (s + 1) % 2, i + (AHEAD + s + 1) // 2)
                    g_load(i * 2 + (AHEAD + s + 1), (s + 1) % 2)
                    v_load(g, g, 0)
                    v_load(g, g, 1)
            for g in (FIRST - 2, FIRST - 1):
                if g + 1 < FIRST:
                    w_load(g + 1, (g + 1) % 2, (g + 1) // 2)
                    g_load(g + 1, (g + 1) % 2)
                v_load(g, g, 0)
                v_load(g, g, 1)
            with sp.Fori(0, (GROUPS - FIRST) // 2) as i:
                for b in range(4):
                    u_load(i * 8 + (SPILL + b), b)
                g = i * 2 + FIRST
                v_load(g, g, 0)
                v_load(g, g, 1)
                w_load(g, 0, i + FIRST // 2)
                w_load(g + 1, 1, i + FIRST // 2)
                u_load(i * 8 + (SPILL + 4), 4)
                u_load(i * 8 + (SPILL + 5), 5)
                v_load(g + 1, g + 1, 0)
                v_load(g + 1, g + 1, 1)
                u_load(i * 8 + (SPILL + 6), 6)
                u_load(i * 8 + (SPILL + 7), 7)
            for k in range(2):
                sp.wait_ge(vraw_free[0], GROUPS + 1)
                sp.dma_start(ln2bc[:, k, :], ln_d[4 + k:5 + k, :].partition_broadcast(P)).then_inc(ln2_in, 16)
            for t in range(TT):
                sp.wait_ge(out_ready, t + 1)
                sp.dma_start(out_d[t], htok[:, t, :]).then_inc(out_stored, 16)
            sp.wait_ge(out_stored, 16 * TT)

        @block.gpsimd
        def _(pool):
            pool.sem_inc(raw_free, 2)
            pool.sem_inc(gw_free, 1)

            def split(raw, hi, lo, ready, free, hi_count):
                nc.gpsimd.tensor_scalar(hi, raw, 1.0, 0.0, ALU.mult, ALU.add).then_inc(tile_hi, 1)
                pool.wait_ge(tile_hi, hi_count)
                nc.gpsimd.tensor_tensor(lo, raw, hi.bitcast(F32), ALU.subtract).then_inc(ready, 1)

            def ring_tile(slot, k_raw, k_ring, hi_count, cols=D):
                pool.wait_ge(raw_in[slot], k_raw)
                pool.wait_ge(tile_used, k_ring)
                pool.sem_inc(apart, 1)
                split(wraw[:, slot, 0:cols], whi[:, slot, 0:cols], wlo[:, slot, 0:cols], tile_split, raw_free, hi_count)
                pool.wait_ge(tile_split, k_ring)
                pool.sem_inc(raw_free, 1)

            def gate_tile(k, hi_count, cols=D):
                pool.wait_ge(gw_in, 16 * (k + 1))
                if k:
                    pool.wait_ge(gw_used, k)
                split(gwraw[:, 0:cols], gwhi[:, 0:cols], gwlo[:, 0:cols], gw_split, gw_free, hi_count)
                pool.wait_ge(gw_split, k + 1)
                pool.sem_inc(gw_free, 1)

            n = 0
            m = 0
            for c in range(C):
                m += 1
                ring_tile(c % 2, 16 * (n // 2 + 1), n + 1, m)
                n += 1
                if c in (1, 5, 7):
                    m += 1
                    gate_tile(c // 2 - (c > 1), m)
            for c in range(POOL_C):
                m += 1
                ring_tile(c % 2, 16 * (n // 2 + 1), n + 1, m)
                n += 1
                if c % 2 == 1:
                    m += 1
                    gate_tile(3 + c // 2, m, D if c == 1 else N)
            for c in range(C):
                m += 1
                ring_tile(c % 2, 16 * (n // 2 + 1), n + 1, m)
                n += 1

            def ring_loop(times, n, m, raw_shift, cols=(D, D)):
                with pool.Fori(0, times) as i:
                    for j in range(2):
                        ring_tile(j, i * 16 + 16 * ((n + raw_shift) // 2 + 1), i * 2 + (n + j + 1),
                                  i * 2 + (m + j + 1), cols[j])
                return n + 2 * times, m + 2 * times

            n, m = ring_loop(C, n, m, 0)
            n, m = ring_loop((C + C // 2) // 2, n, m, 0)
            assert n == T_Q
            for c in range(C):
                m += 1
                if c == 0:
                    pool.wait_ge(tile_used, T_Y + 2)
                if c == C // 2:
                    pool.wait_ge(tile_used, T_Q + 2)
                pool.wait_ge(raw_in[c % 2], 16 * ((n + c) // 2 + 1))
                half, k = c // (C // 2), c % (C // 2)
                split(wraw[:, c % 2, :], wo_hi[half][:, k, :], wo_lo[half][:, k, :], wo_split, raw_free, m)
                pool.wait_ge(wo_split, c + 1)
                pool.sem_inc(raw_free, 1)
            n, m = ring_loop(HEADS, n, m, RAW_WO)
            n, m = ring_loop(GB * AHEAD // 2, n, m, RAW_WO)
            ring_loop((KEYS - GB * AHEAD) // 2, n, m, RAW_WO)

        @block.tensor
        def _(pe):
            pe.sem_inc(tile_used, 2)
            pe.sem_inc(oe_done, 16)

            def three(out, lhi, llo, rhi, rlo, start, stop):
                nc.tensor.matmul(out, lhi, rhi, start=start, stop=False)
                nc.tensor.matmul(out, lhi, rlo, start=False, stop=False)
                return nc.tensor.matmul(out, llo, rhi, start=False, stop=stop)

            def tile_product(slot, outs, rhs, chunks=C):
                for c in range(chunks):
                    w = slice(c * P, (c + 1) * P)
                    for out, cols in outs:
                        mm = three(out, whi[:, slot, w], wlo[:, slot, w], rhs[0][:, c, cols], rhs[1][:, c, cols],
                                   c == 0, c == chunks - 1)
                return mm

            pe.wait_ge(consts_in, 48)

            def h_transposes(t):
                pe.wait_ge(h_ready, t + 1)
                rows = META if t == 0 else P
                for hh in range(2):
                    u = 2 * t + hh
                    for k in range(4):
                        c = 4 * hh + k
                        s = hmeta[0:META, c * P:(c + 1) * P] if t == 0 else htok[:, t - 1, c * P:(c + 1) * P]
                        mm = nc.tensor.transpose(ps[:, TR_BANK[u], k * P:k * P + rows], s, ident[0:rows, 0:rows])
                    mm.then_inc(tr_done, 1)

            def x_chunk(n, halves=(0, 1)):
                pe.wait_ge(tile_split, n + 1)
                if n >= 2:
                    pe.wait_ge(x_evac, n - 1)
                b = 2 * (n % 2)
                outs = [(ps[:, b + k, 0:TH], slice(k * TH, (k + 1) * TH)) for k in halves]
                mm = tile_product(n % 2, outs, (ht_hi, ht_lo))
                if 1 in halves:
                    mm.then_inc(tile_used, 1)

            def gates_of(n):
                pe.wait_ge(gw_split, n + 1)
                pe.wait_ge(xc_split, 2 * n + 2)
                for o in range(4):
                    k = 4 * n + o
                    if k >= 2:
                        pe.wait_ge(ri_evac, k - 1)
                    b = 4 + 2 * (k % 2)
                    for kc in range(2):
                        w = slice((o // 2) * 512 + kc * 256 + (o % 2) * P, (o // 2) * 512 + kc * 256 + (o % 2) * P + P)
                        x = (2 * n + kc) % 4
                        for half in range(2):
                            cols = slice(half * TH, (half + 1) * TH)
                            mm = three(ps[:, b + half, 0:TH], gwhi[:, w], gwlo[:, w], xc_hi[:, x, cols],
                                       xc_lo[:, x, cols], kc == 0, kc == 1)
                    mm.then_inc(ri_done, 1)
                pe.wait_ge(ri_done, 4 * n + 4)
                pe.sem_inc(gw_used, 1)

            for t in range(3):
                h_transposes(t)
            pe.wait_ge(ht_split, 6)
            x_chunk(0, (0,))
            h_transposes(3)
            x_chunk(1, (0,))
            h_transposes(4)
            pe.wait_ge(ht_split, 2 * (TT + 1))
            x_chunk(0, (1,))
            x_chunk(1, (1,))
            for n in range(3):
                x_chunk(2 * n + 2)
                x_chunk(2 * n + 3)
                gates_of(n)
            x_chunk(8)
            x_chunk(9)
            gates_of(3)
            x_chunk(10)
            x_chunk(11)

            def gate_chunk(c):
                pe.wait_ge(tile_split, T_GA + c + 1)
                if c == 0:
                    pe.wait_ge(x_evac, 12)
                if c >= 4:
                    pe.wait_ge(mixed_split, c - 3)
                tile_product(c % 2, [(ps[:, c, :], slice(META, T))], (ht_hi, ht_lo)).then_inc(tile_used, 1)

            for c in range(2):
                gate_chunk(c)
            pe.wait_ge(gw_split, 5)
            pe.wait_ge(ri_evac, 16)
            for g in range(POOL_GROUPS):
                pe.wait_ge(pl_split, g + 1)
                three(ps[:, 4 + g, :], gwhi[:, g * P:(g + 1) * P], gwlo[:, g * P:(g + 1) * P],
                      pl_hi[:, g, :], pl_lo[:, g, :], True, True).then_inc(mix_done, 1)
            for c in range(2, C):
                gate_chunk(c)

            pe.wait_ge(gelu_done, 2)
            with pe.Fori(0, C) as i:
                for j in range(2):
                    pe.wait_ge(tile_split, i * 2 + (T_GL + j + 1))
                    pe.wait_ge(gl_free, i * 2 + (j + 1))
                    tile_product(j, [(ps[:, j, :], slice(META, T))], (ht_hi, ht_lo)).then_inc(tile_used, 1)
            pe.wait_ge(gelu_done, C)
            pe.wait_ge(ya_split, C)
            pe.wait_ge(mixed_split, POOL_C)
            with pe.Fori(0, C // 4) as i:
                for j in range(2):
                    for k in range(2):
                        pe.wait_ge(y_free, i * 4 + (2 * j + k + 1))
                        pe.wait_ge(tile_split, i * 6 + (T_Y + 3 * j + k + 1))
                        if (j, k) == (1, 0):
                            pe.wait_ge(gl_free, 2 + 2 * C)
                        tile_product((j + k) % 2, [(ps[:, A_BANK[2 * j + k], :], slice(0, N))], (ya_hi, ya_lo))\
                            .then_inc(tile_used, 1)
                    pe.wait_ge(tile_split, i * 6 + (T_Y + 3 * j + 3))
                    for k in range(2):
                        for c in range(POOL_C):
                            w = slice((k * POOL_C + c) * P, (k * POOL_C + c + 1) * P)
                            mm = three(ps[:, B_BANK[2 * j + k], :], whi[:, j, w], wlo[:, j, w],
                                       mixed_hi[:, c, :], mixed_lo[:, c, :], c == 0, c == POOL_C - 1)
                    mm.then_inc(tile_used, 1)

            def o_product(half, t, first):
                for k in range(C // 2):
                    c = half * (C // 2) + k
                    if first:
                        pe.wait_ge(wo_split, c + 1)
                        pe.wait_ge(mg_split, c + 1)
                    rows = slice(t * P, (t + 1) * P)
                    for dh in range(2):
                        cols = slice(dh * HD, (dh + 1) * HD)
                        mm = three(ps[:, 2 * t + dh, :], mg_hi[:, c, rows], mg_lo[:, c, rows],
                                   wo_hi[half][:, k, cols], wo_lo[half][:, k, cols], c == 0, c == C - 1)
                if half == 1:
                    mm.then_inc(o_done, 1)

            def h1_transposes(t):
                pe.wait_ge(h1_ready, t + 1)
                for hh in range(2):
                    for k in range(4):
                        c = 4 * hh + k
                        mm = nc.tensor.transpose(ps[:, 2 * t + hh, k * P:(k + 1) * P],
                                                 htok[:, t, c * P:(c + 1) * P], ident[:, :])
                    mm.then_inc(tr1_done, 1)

            for n, t in enumerate((1, 2, 0, 3)):
                pe.wait_ge(y_free, 4 + (C - 2 if n < 2 else C))
                o_product(0, t, n == 0)
            for t in range(TT - 1):
                o_product(1, t, t == 0)
            h1_transposes(0)
            h1_transposes(1)
            o_product(1, TT - 1, False)
            h1_transposes(2)

            def scores(i):
                for j in range(2):
                    pe.wait_ge(q_free, i * 2 + (j + 3))
                    pe.wait_ge(s_free, i * 2 + (j + 1))
                    for t in range(TT):
                        mm = nc.tensor.matmul(ps[:, 2 + j, t * KEYS:(t + 1) * KEYS], qf[:, j, t * P:(t + 1) * P],
                                              keys[:, bass.ds(i * 2 + j, 1), :].rearrange("p a k -> p (a k)"),
                                              start=True, stop=True)
                    mm.then_inc(s_done, 1)

            pe.wait_ge(h1_split, TT)
            for half in range(2):
                for j in range(2):
                    if half == 0:
                        pe.wait_ge(tile_split, T_Q + j + 1)
                    cols = slice(half * (N // 2), (half + 1) * (N // 2))
                    mm = tile_product(j, [(ps[:, j, cols], cols)], (h1_hi, h1_lo))
                    if half == 1:
                        mm.then_inc(tile_used, 1)
                if half == 0:
                    h1_transposes(3)
                    pe.wait_ge(h1_split, 2 * TT)
            pe.wait_ge(keys_in, 16)
            pe.sem_inc(s_done, 2)
            scores(0)
            with pe.Fori(1, HEADS) as i:
                for j in range(2):
                    pe.wait_ge(tile_split, i * 2 + (T_Q + j + 1))
                    pe.wait_ge(q_free, i * 2 + (j + 1))
                    tile_product(j, [(ps[:, j, :], slice(0, N))], (h1_hi, h1_lo)).then_inc(tile_used, 1)
                scores(i)

            def hidden(slot, bank, tile):
                pe.wait_ge(tile_split, tile + 1)
                tile_product(slot, [(ps[:, bank, :], slice(0, N))], (h1_hi, h1_lo)).then_inc(tile_used, 1)

            with pe.Fori(0, GB * AHEAD // 2) as i:
                for j in range(2):
                    pe.wait_ge(z_free, i * 2 + (j + 1))
                    hidden(j, 4 + j, i * 2 + (T_U + j))

            with pe.Fori(0, PRE // 2) as i:
                for j in range(2):
                    pe.wait_ge(z_free, i * 2 + (GB * AHEAD + j + 1))
                    hidden(j, 4 + j, i * 2 + (T_US + j))

            pe.wait_ge(sel_ready, 1)
            for k in range(3):
                bank = 6 + k if k < 2 else 0
                if k == 2:
                    pe.wait_ge(q_free, 2 + 2 * HEADS)
                for t in range(TT):
                    mm = nc.tensor.transpose(ps[:, bank, t * P:(t + 1) * P], sel[:, k, t * SEL:(t + 1) * SEL],
                                             ident[:, :])
                mm.then_inc(selT_done, 1)

            for b in range(PRE, PRE + MID):
                pe.wait_ge(z_free, GB * AHEAD + b + 1)
                hidden(b % 2, 4 + b % 2, T_US + b)

            pe.wait_ge(selT_ready, 3)
            pe.wait_ge(s_free, 2 + 2 * HEADS)
            pe.sem_inc(quad_done, 4)
            with pe.Fori(0, WCHUNKS // 2) as i:
                for s in range(2):
                    for q in range(WT // 4):
                        k = s * 8 + q
                        pe.wait_ge(oh_ready, i * 8 + (k // 2 + 2))
                        pe.wait_ge(quad_free, i * 16 + (k + 1))
                        o, a = (k // 2) % 2, k % 2
                        for t in range(4):
                            for part in range(3):
                                mm = nc.tensor.matmul(ps[:, q % 4, t * P:(t + 1) * P], oh2[:, o, a, :, t],
                                                      ohw[:, o, part, a, :, t], start=part == 0, stop=part == 2)
                        mm.then_inc(quad_done, 1)
                        if q % 4 == 3:
                            b = k // 4
                            pe.wait_ge(z_free, i * BUILD + (GB * AHEAD + PRE + MID + b + 1))
                            hidden(b % 2, 4 + b % 2, i * BUILD + (T_US + PRE + MID + b))
            for b in range(SPILL - POST, SPILL):
                pe.wait_ge(z_free, GB * AHEAD + b + 1)
                hidden(b % 2, 4 + b % 2, T_US + b)

            def mix_group(slot, g, order, banks):
                pe.wait_ge(a_split, g + 1)
                halves = []
                for p, (dh, t) in enumerate(order):
                    if dh not in halves:
                        halves.append(dh)
                        pe.wait_ge(v_split, g * 2 + (dh + 1))
                    pe.wait_ge(oe_free, g * 8 + (p + 9 - banks))
                    rows = slice(t * P, (t + 1) * P)
                    bank = (4 + p) % 8 if banks == 8 else 4 + p % 4
                    for b in range(GB):
                        mm = three(ps[:, bank, :], ahi[:, slot, b, rows], alo[:, slot, b, rows],
                                   vhi[:, dh, b, :], vlo[:, dh, b, :], b == 0, b == GB - 1)
                    mm.then_inc(oe_done, 1)

            pe.wait_ge(z_free, 2 + GB * FIRST)
            pe.wait_ge(quad_free, 4 + N // 4)
            with pe.Fori(0, FIRST // 2) as i:
                for s in range(2):
                    mix_group(s, i * 2 + s, BY_HALF, 8)
            pe.wait_ge(oe_free, 8 + 8 * FIRST - 2)
            with pe.Fori(0, (GROUPS - FIRST) // 2) as i:
                for b in range(2 * GB):
                    pe.wait_ge(z_free, i * 8 + (GB * FIRST + b + 1))
                    hidden(b % 2, b % 2, i * 8 + (T_UD + b))
                for s in range(2):
                    mix_group(s, i * 2 + (FIRST + s), (BY_HALF, BY_TILES)[s], 4)

        @block.scalar
        def _(act):
            ch = Chain(act, act_step)
            act.sem_inc(gl_free, 2)
            act.sem_inc(q_free, 2)
            act.sem_inc(s_free, 2)
            act.sem_inc(z_free, 2)
            act.sem_inc(quad_free, 4)

            def used(tile):
                act.wait_ge(tile_used, tile + 3)

            def in_deviation(n):
                act.wait_ge(var_ready, n + 1)
                nc.scalar.activation(sdev[:, IN_PARTS[n]], veps[:, IN_PARTS[n]], ACT.Sqrt).then_inc(sd_ready, 1)

            in_deviation(0)
            for u in range(2 * (TT + 1)):
                if u == 2:
                    in_deviation(1)
                t, hh = u // 2, u % 2
                act.wait_ge(tr_done, u + 1)
                rows = META if t == 0 else P
                off = 0 if t == 0 else META + (t - 1) * P
                nc.scalar.activation(ht_hi[:, 4 * hh:4 * hh + 4, off:off + rows],
                                     ps[:, TR_BANK[u], :].rearrange("p (c t) -> p c t", c=4)[:, :, 0:rows],
                                     ACT.Copy).then_inc(ht_hi_done, 1)

            act.wait_ge(consts_in, 48)
            ch.done(nc.scalar.activation(lam[:, 0, :], par[:, LL:LL + C], ACT.Abs))
            ch.wait()
            nc.scalar.activation(lam[:, 1, :], lam[:, 0, :], ACT.Exp, scale=-1.0).then_inc(lam_e, 1)

            def x_out(n):
                used(n)
                src = ps[:, 2 * (n % 2):2 * (n % 2) + 2, 0:TH]
                if n < C:
                    if n >= 2:
                        act.wait_ge(conv_done, n - 1)
                    dst = xrp[:, n % 2, CONV - 1:].rearrange("p (h t) -> p h t", h=2)
                else:
                    dst = xp[:, n - C, :].rearrange("p (h t) -> p h t", h=2)
                nc.scalar.activation(dst, src, ACT.Copy).then_inc(x_evac, 1)

            def xc_high(c):
                act.wait_ge(conv_done, c + 1)
                if c >= 4:
                    act.wait_ge(gw_used, (c - 4) // 2 + 1)
                nc.scalar.activation(xc_hi[:, c % 4, :], xc[:, c % 4, :], ACT.Copy).then_inc(xc_hi_done, 1)

            def gates_out(n):
                for o in range(4):
                    k = 4 * n + o
                    act.wait_ge(ri_done, k + 1)
                    c = 2 * n + o % 2
                    dst = (R if o < 2 else I)[:, c, :].rearrange("p (h t) -> p h t", h=2)
                    bias = par[:, (BR if o < 2 else BI) + c:(BR if o < 2 else BI) + c + 1]
                    b = 4 + 2 * (k % 2)
                    nc.scalar.activation(dst, ps[:, b:b + 2, 0:TH], ACT.Sigmoid, bias=bias).then_inc(ri_evac, 1)

            x_out(0)
            x_out(1)
            xc_high(0)
            xc_high(1)
            for n in range(3):
                x_out(2 * n + 2)
                x_out(2 * n + 3)
                gates_out(n)
                xc_high(2 * n + 2)
                xc_high(2 * n + 3)
            x_out(8)
            x_out(9)
            gates_out(3)
            x_out(10)
            x_out(11)
            for g in range(POOL_GROUPS):
                act.wait_ge(pooled, g + 1)
                nc.scalar.activation(pl_hi[:, g, :], (psa, psb)[g % 2][:, META:T], ACT.Copy).then_inc(pl_hi_done, 1)
            for g in range(POOL_GROUPS):
                act.wait_ge(mix_done, g + 1)
                nc.scalar.activation(mixed_hi[:, g, :], ps[:, 4 + g, :], ACT.Identity,
                                     scale=par[:, PSC + g:PSC + g + 1]).then_inc(mixed_hi_done, 1)

            act.wait_ge(lam_ready, 1)
            act.wait_ge(gw_used, 4)
            act.wait_ge(mixed_split, POOL_C)
            for c in range(C):
                nc.scalar.activation(A[:, c, :], R[:, c, :], ACT.Exp, scale=lam[:, 8, c:c + 1]).then_inc(act_step, 1)
                ch.n += 1
                ch.wait()
                nc.scalar.activation(R[:, c, :], R[:, c, :], ACT.Tanh, scale=lam[:, 9, c:c + 1]).then_inc(at_done, 1)
            for c in range(C):
                act.wait_ge(m_done, c + 1)
                nc.scalar.activation(R[:, c, :], R[:, c, :], ACT.Sqrt).then_inc(mult_done, 1)

            def y_high(c):
                act.wait_ge(yf_done, c + 1)
                nc.scalar.activation(ya_hi[:, c, :], yf[:, c % 2, :], ACT.Copy).then_inc(ya_hi_done, 1)

            for c in range(C):
                used(T_GA + c)
                if c >= 2:
                    act.wait_ge(yf_done, c - 1)
                nc.scalar.activation(gel[:, c % 2, :], ps[:, c, :], ACT.Gelu_apprx_tanh).then_inc(gelu_done, 1)
                if c >= 1:
                    y_high(c - 1)
            y_high(C - 1)
            act.wait_ge(ya_split, C)
            with act.Fori(0, C) as i:
                for j in range(2):
                    act.wait_ge(tile_used, i * 2 + (T_GL + j + 3))
                    act.sem_inc(apart, 1)
                    nc.scalar.activation(gates[:, bass.ds(i * 2 + j, 1), :].rearrange("p a n -> p (a n)"),
                                         ps[:, j, :], ACT.Sigmoid).then_inc(gl_free, 1)
            with act.Fori(0, C // 2) as i:
                for j in range(2):
                    act.wait_ge(mf_done, i * 2 + (j + 1))
                    act.sem_inc(apart, 1)
                    nc.scalar.activation(mg_hi[:, bass.ds(i * 2 + j, 1), :].rearrange("p a n -> p (a n)"),
                                         m1[:, j, :], ACT.Copy).then_inc(mg_hi_done, 1)
            def deviation(t):
                act.wait_ge(var_ready, SD + t + 1)
                nc.scalar.activation(sdev[:, t:t + 1], veps[:, t:t + 1], ACT.Sqrt).then_inc(sd_ready, 1)

            def h1_high(t):
                for hh in range(2):
                    u = 2 * t + hh
                    act.wait_ge(tr1_done, u + 1)
                    nc.scalar.activation(h1_hi[:, 4 * hh:4 * hh + 4, t * P:(t + 1) * P],
                                         ps[:, u, :].rearrange("p (c t) -> p c t", c=4), ACT.Copy)\
                        .then_inc(h1_hi_done, 1)

            for t in range(3):
                deviation(t)
            h1_high(0)
            h1_high(1)
            deviation(3)
            h1_high(2)
            h1_high(3)
            for t in range(TT):
                nc.scalar.mul(htok[:, t, :], htok[:, t, :], ALPHA).then_inc(acc_ready, 1)

            with act.Fori(0, HEADS) as i:
                for j in range(2):
                    act.wait_ge(tile_used, i * 2 + (T_Q + j + 3))
                    act.wait_ge(s_done, i * 2 + (j + 1))
                    nc.scalar.activation(qf[:, j, :], ps[:, j, :], ACT.Copy).then_inc(q_free, 1)
                for j in range(2):
                    act.wait_ge(s_done, i * 2 + (j + 3))
                    act.sem_inc(apart, 1)
                    nc.scalar.activation(S_all[:, bass.ds(i * 2 + j, 1)].rearrange("p a t k -> p (a t k)"),
                                         ps[:, 2 + j, :], ACT.Copy).then_inc(s_free, 1)
            with act.Fori(0, GB * AHEAD // 2) as i:
                for j in range(2):
                    act.wait_ge(tile_used, i * 2 + (T_U + j + 3))
                    act.sem_inc(apart, 1)
                    nc.scalar.activation(G[:, bass.ds(i * 2 + j, 1), :].rearrange("p a n -> p (a n)"),
                                         ps[:, 4 + j, :], ACT.Gelu_apprx_tanh).then_inc(z_free, 1)

            def hidden_out(b, j, stored):
                act.wait_ge(tile_used, b + (T_US + 3))
                act.wait_ge(gst_stored[j % 2], stored)
                nc.scalar.activation(gst[:, j % 2, :], ps[:, 4 + j % 2, :], ACT.Gelu_apprx_tanh).then_inc(z_free, 1)

            with act.Fori(0, (PRE - EXP_AHEAD) // 2) as i:
                for j in range(2):
                    hidden_out(i * 2 + j, j, i * 16 + 16)
            act.wait_ge(cmax_ready, 1)
            nc.scalar.activation(cv_all[:, :, :, :], cv_all[:, :, :, :], ACT.Exp).then_inc(cexp_done, 1)
            for b in range(PRE - EXP_AHEAD, PRE):
                hidden_out(b, b, 16 * (b // 2 + 1))
            for k in range(3):
                act.wait_ge(selT_done, k + 1)
                nc.scalar.activation(selT[:, k, :], ps[:, 6 + k if k < 2 else 0, :], ACT.Copy).then_inc(selT_ready, 1)
            for b in range(PRE, PRE + MID):
                hidden_out(b, b, 16 * (b // 2 + 1))
            with act.Fori(0, WCHUNKS // 2) as i:
                for s in range(2):
                    act.wait_ge(w_stored[s], i * 16 + 16)
                    for q in range(WT // 4):
                        act.wait_ge(quad_done, i * 16 + (s * 8 + q + 5))
                        nc.scalar.activation(wst[:, s, :, 4 * q:4 * q + 4],
                                             ps[:, q % 4, :].rearrange("p (t k) -> p k t", t=4), ACT.Copy)\
                            .then_inc(quad_free, 1)
                        if q % 4 == 3:
                            b = 2 * s + q // 4
                            hidden_out(i * BUILD + (PRE + MID + b), b,
                                       i * 8 * BUILD + 16 * ((PRE + MID) // 2 + 1 + b // 2))

            def v_high(k, dh, last=BY_HALF):
                act.wait_ge(v_in[dh], k * 16 + 16)
                uses = 1 + max(p for p, (h, t) in enumerate(last) if h == dh)
                act.wait_ge(oe_done, k * 8 + (8 + uses))
                nc.scalar.activation(vhi[:, dh], vraw[:, dh], ACT.Copy).then_inc(v_hi, 1)

            def a_high(k, slot, src):
                act.wait_ge(a_ready, k + 1)
                act.sem_inc(apart, 1)
                nc.scalar.activation(ahi[:, slot], src, ACT.Copy).then_inc(a_hi, 1)

            for b in range(SPILL - POST, SPILL):
                hidden_out(b, b, 16 * (b // 2 + 1))
                if b == SPILL - 5:
                    v_high(0, 0)
                    v_high(0, 1)
                if b == SPILL - 3:
                    a_high(0, 0, G[:, 0:GB, :])

            def next_group(k, slot, first_block):
                a_high(k, slot, G[:, first_block:first_block + GB, :])
                v_high(k, 0)
                v_high(k, 1)

            for k in range(1, AHEAD + 1):
                next_group(k, k % 2, k * GB if k < AHEAD else 0)
            with act.Fori(0, SPILLED // 2 - 1) as i:
                next_group(i * 2 + (AHEAD + 1), 1, GB)
                next_group(i * 2 + (AHEAD + 2), 0, 0)
            next_group(FIRST - 1, 1, GB)
            with act.Fori(0, (GROUPS - FIRST) // 2) as i:
                g = i * 2 + FIRST
                v_high(g, 0, BY_TILES)
                v_high(g, 1, BY_TILES)
                for b in range(2 * GB):
                    act.wait_ge(tile_used, i * 8 + (T_UD + b + 3))
                    if b % GB == 0:
                        act.wait_ge(a_split, i * 2 + (FIRST - 1 + b // GB))
                    nc.scalar.activation(G[:, b, :], ps[:, b % 2, :], ACT.Gelu_apprx_tanh).then_inc(z_free, 1)
                    if b == GB:
                        a_high(g, 0, G[:, 0:GB, :])
                a_high(g + 1, 1, G[:, GB:2 * GB, :])
                v_high(g + 1, 0)
                v_high(g + 1, 1)
            for t in range(TT):
                act.wait_ge(var_ready, SD + TT + t + 1)
                nc.scalar.activation(sdev[:, t:t + 1], veps[:, t:t + 1], ACT.Sqrt).then_inc(sd_ready, 1)

        @block.vector
        def _(dve):
            ch = Chain(dve, dve_step)
            dve.sem_inc(y_free, 4)
            dve.sem_inc(vraw_free[0], 1)
            dve.sem_inc(vraw_free[1], 1)
            dve.sem_inc(w_free[0], 1)
            dve.sem_inc(w_free[1], 1)
            dve.sem_inc(oe_free, 8)
            V = nc.vector

            def norm_stats(row, rows, k):
                for h in range(2):
                    ch.done(V.bn_stats(stats[0:rows, k, 6 * h:6 * h + 6], row[:, h * HD:(h + 1) * HD]))
                ch.wait()
                ch.done(V.bn_aggr(mv[0:rows, k, :], stats[0:rows, k, :]))

            def norm_apply(row, rows, k, bc, signal):
                ch.done(V.scalar_tensor_tensor(row, row, mv[0:rows, k, 0:1], bc[0:rows, 0, :], ALU.subtract, ALU.mult))
                ch.wait()
                V.scalar_tensor_tensor(row, row, rstd[0:rows, k:k + 1], bc[0:rows, 1, :],
                                       ALU.mult, ALU.add).then_inc(signal, 1)

            ch.done(V.memset(mv[:, :, :], 1.0))
            ch.done(V.memset(xrp[:, :, 0:CONV - 1], 0.0))
            ch.wait()
            rows_of = [(hmeta[0:META, :], META)] + [(htok[:, t, :], P) for t in range(TT)]
            def ht_low(u):
                t, hh = u // 2, u % 2
                rows = META if t == 0 else P
                off = 0 if t == 0 else META + (t - 1) * P
                dve.wait_ge(ht_hi_done, u + 1)
                V.tensor_tensor(ht_lo[:, 4 * hh:4 * hh + 4, off:off + rows],
                                ps[:, TR_BANK[u], :].rearrange("p (c t) -> p c t", c=4)[:, :, 0:rows],
                                ht_hi[:, 4 * hh:4 * hh + 4, off:off + rows].bitcast(F32),
                                ALU.subtract).then_inc(ht_split, 1)

            def in_stats(n):
                for k in range(TT + 1)[IN_PARTS[n]]:
                    dve.wait_ge(x_in[k], 16)
                    norm_stats(*rows_of[k], k)
                ch.wait()
                V.tensor_scalar(veps[:, IN_PARTS[n]], mv[:, IN_PARTS[n], 1], EPS, None, ALU.add).then_inc(var_ready, 1)

            def in_deviations(n):
                dve.wait_ge(sd_ready, n + 1)
                ch.done(V.reciprocal(rstd[:, IN_PARTS[n]], sdev[:, IN_PARTS[n]]))
                ch.wait()

            in_stats(0)
            in_deviations(0)
            dve.wait_ge(ln_in, 32)
            for k, (row, rows) in enumerate(rows_of):
                if k == 2:
                    in_stats(1)
                if k == 3:
                    in_deviations(1)
                norm_apply(row, rows, k, lnbc, h_ready)
                if k >= 1:
                    ht_low(2 * k - 2)
                    ht_low(2 * k - 1)
            ht_low(2 * TT)
            ht_low(2 * TT + 1)

            dve.wait_ge(lam_e, 1)
            e, s, z, q = lam[:, 1, :], lam[:, 3, :], lam[:, 4, :], lam[:, 5, :]
            ch.done(V.tensor_scalar(lam[:, 2, :], e, 2.0, None, ALU.add))
            ch.wait()
            ch.done(V.reciprocal(s, lam[:, 2, :]))
            ch.wait()
            ch.done(V.tensor_tensor(s, s, e, ALU.mult))
            ch.wait()
            ch.done(V.tensor_tensor(z, s, s, ALU.mult))
            ch.wait()
            ch.done(V.tensor_scalar(q, z, 1.0 / 17.0, None, ALU.mult))
            for k in (15, 13, 11, 9, 7, 5, 3):
                ch.wait()
                ch.done(V.scalar_tensor_tensor(q, q, 1.0 / k, z, ALU.add, ALU.mult))
            ch.wait()
            ch.done(V.scalar_tensor_tensor(q, q, 1.0, s, ALU.add, ALU.mult))
            ch.done(V.tensor_scalar(lam[:, 6, :], par[:, LL:LL + C], 0.0, LRU_C, ALU.min, ALU.mult))
            ch.wait()
            ch.done(V.scalar_tensor_tensor(lam[:, 8, :], q, -2.0 * LRU_C, lam[:, 6, :], ALU.mult, ALU.add))
            ch.wait()
            V.tensor_scalar(lam[:, 9, :], lam[:, 8, :], -1.0, None, ALU.mult).then_inc(lam_ready, 1)

            def conv(c):
                dve.wait_ge(x_evac, c + 1)
                if c >= 4:
                    ch.wait()
                    dve.wait_ge(xc_split, c - 3)
                x, y = xrp[:, c % 2, :], xc[:, c % 4, :]
                w = [par[:, CW + 4 * c + k:CW + 4 * c + k + 1] for k in range(CONV)]
                ch.done(V.tensor_scalar(y, x[:, CONV - 1:], w[CONV - 1], par[:, CB + c:CB + c + 1], ALU.mult, ALU.add))
                for k in range(CONV - 2, -1, -1):
                    ch.wait()
                    ins = V.scalar_tensor_tensor(y, x[:, k:k + T], w[k], y, ALU.mult, ALU.add)
                    if k:
                        ch.done(ins)
                    else:
                        ins.then_inc(conv_done, 1)

            def xc_low(c):
                dve.wait_ge(xc_hi_done, c + 1)
                V.tensor_tensor(xc_lo[:, c % 4, :], xc[:, c % 4, :], xc_hi[:, c % 4, :].bitcast(F32),
                                ALU.subtract).then_inc(xc_split, 1)

            def gated_input(n):
                dve.wait_ge(ri_evac, 4 * n + 4)
                for c in (2 * n, 2 * n + 1):
                    ch.done(V.tensor_tensor(I[:, c, :], I[:, c, :], xc[:, c % 4, :], ALU.mult))

            conv(0)
            conv(1)
            xc_low(0)
            xc_low(1)
            for n in range(3):
                conv(2 * n + 2)
                conv(2 * n + 3)
                xc_low(2 * n + 2)
                xc_low(2 * n + 3)
                gated_input(n)
            gated_input(3)

            for g in range(POOL_GROUPS):
                dve.wait_ge(x_evac, C + g + 1)
                if g >= 2:
                    dve.wait_ge(pl_hi_done, g - 1)
                if g >= 1:
                    dve.wait_ge(pl_hi_done, g)
                    V.tensor_tensor(pl_lo[:, g - 1, :], (psa, psb)[(g - 1) % 2][:, META:T],
                                    pl_hi[:, g - 1, :].bitcast(F32), ALU.subtract).then_inc(pl_split, 1)
                    dve.wait_ge(pl_split, g)
                levels = g + 1
                x0 = xp[:, g, :]
                src = x0
                for k in range(1, levels + 1):
                    start = META - ((1 << levels) - (1 << k))
                    sh = 1 << (k - 1)
                    dst = (psb, psa)[(g + levels - k) % 2]
                    ch.done(V.tensor_tensor(dst[:, start:T], src[:, start:T], src[:, start - sh:T - sh], ALU.add))
                    ch.wait()
                    src = dst
                out = (psa, psb)[g % 2]
                V.scalar_tensor_tensor(out[:, META:T], src[:, META:T], 1.0 / (1 << levels), x0[:, META:T],
                                       ALU.mult, ALU.subtract).then_inc(pooled, 1)
            g = POOL_GROUPS
            dve.wait_ge(pl_hi_done, g)
            V.tensor_tensor(pl_lo[:, g - 1, :], (psa, psb)[(g - 1) % 2][:, META:T],
                            pl_hi[:, g - 1, :].bitcast(F32), ALU.subtract).then_inc(pl_split, 1)
            for g in range(POOL_GROUPS):
                dve.wait_ge(mixed_hi_done, g + 1)
                V.scalar_tensor_tensor(mixed_lo[:, g, :], ps[:, 4 + g, :], par[:, PSC + g:PSC + g + 1],
                                       mixed_hi[:, g, :].bitcast(F32), ALU.mult, ALU.subtract).then_inc(mixed_split, 1)

            for c in range(C):
                dve.wait_ge(at_done, c + 1)
                if c >= 2:
                    dve.wait_ge(m_done, c - 1)
                tmp = (yf, gel)[c % 2].rearrange("p a n -> p (a n)")[:, 0:T]
                ch.done(V.tensor_tensor(tmp, A[:, c, :], A[:, c, :], ALU.mult))
                ch.wait()
                V.scalar_tensor_tensor(R[:, c, :], tmp, 1.0, R[:, c, :], ALU.add, ALU.mult).then_inc(m_done, 1)
            for c in range(C):
                dve.wait_ge(mult_done, c + 1)
                ch.done(V.tensor_tensor(I[:, c, :], I[:, c, :], R[:, c, :], ALU.mult))
                ch.wait()
                ch.done(V.tensor_tensor_scan(R[:, c, :], A[:, c, :], I[:, c, :], 0.0, ALU.mult, ALU.add))
            def ya_low(c):
                dve.wait_ge(ya_hi_done, c + 1)
                V.tensor_tensor(ya_lo[:, c, :], yf[:, c % 2, :], ya_hi[:, c, :].bitcast(F32),
                                ALU.subtract).then_inc(ya_split, 1)

            for c in range(C):
                dve.wait_ge(gelu_done, c + 1)
                if c == 0:
                    ch.wait()
                if c >= 2:
                    dve.wait_ge(ya_split, c - 1)
                V.tensor_tensor(yf[:, c % 2, :], R[:, c, META:T], gel[:, c % 2, :], ALU.mult).then_inc(yf_done, 1)
                if c >= 1:
                    ya_low(c - 1)
            ya_low(C - 1)

            dve.wait_ge(gl_free, 2 + 2 * C)
            dve.wait_ge(ya_split, C)
            with dve.Fori(0, C // 4) as i:
                ch.enter(i, 12)
                for jj in range(4):
                    m, j = i * 4 + jj, jj % 2
                    dve.wait_ge(tile_used, i * 6 + (T_Y + 3 * (jj // 2) + 5))
                    dve.sem_inc(apart, 1)
                    for dst, off, bank in ((m1, 0, A_BANK[jj]), (m2, C, B_BANK[jj])):
                        ch.done(V.tensor_tensor(dst[:, j, :],
                                                gates[:, bass.ds(m + off, 1), :].rearrange("p a n -> p (a n)"),
                                                ps[:, bank, :], ALU.mult))
                    ch.wait()
                    dve.sem_inc(y_free, 1)
                    V.tensor_tensor(m1[:, j, :], m1[:, j, :], m2[:, j, :], ALU.add).then_inc(mf_done, 1)
                    dve.wait_ge(mg_hi_done, i * 4 + (jj + 1))
                    dve.sem_inc(apart, 1)
                    at_m = bass.ds(m, 1)
                    ch.done(V.tensor_tensor(mg_lo[:, at_m, :].rearrange("p a n -> p (a n)"), m1[:, j, :],
                                            mg_hi[:, at_m, :].rearrange("p a n -> p (a n)").bitcast(F32),
                                            ALU.subtract))
                    ch.wait()
                    dve.sem_inc(mg_split, 1)
                ch.leave(C // 4)

            dve.wait_ge(ln1_in, 32)

            def first_norm(t):
                dve.wait_ge(o_done, t + 1)
                for dh in range(2):
                    cols = slice(dh * HD, (dh + 1) * HD)
                    ch.done(V.scalar_tensor_tensor(htok[:, t, cols], htok[:, t, cols], ALPHA, ps[:, 2 * t + dh, :],
                                                   ALU.mult, ALU.add))
                ch.wait()
                norm_stats(htok[:, t, :], P, t)
                ch.wait()
                V.tensor_scalar(veps[:, t:t + 1], mv[:, t, 1:2], EPS, None, ALU.add).then_inc(var_ready, 1)
                dve.wait_ge(sd_ready, SD + t + 1)
                ch.done(V.reciprocal(rstd[:, t:t + 1], sdev[:, t:t + 1]))
                ch.wait()
                norm_apply(htok[:, t, :], P, t, lnbc, h1_ready)

            def h1_low(t):
                for hh in range(2):
                    u = 2 * t + hh
                    dve.wait_ge(h1_hi_done, u + 1)
                    V.tensor_tensor(h1_lo[:, 4 * hh:4 * hh + 4, t * P:(t + 1) * P],
                                    ps[:, u, :].rearrange("p (c t) -> p c t", c=4),
                                    h1_hi[:, 4 * hh:4 * hh + 4, t * P:(t + 1) * P].bitcast(F32),
                                    ALU.subtract).then_inc(h1_split, 1)

            for t in range(3):
                first_norm(t)
            h1_low(0)
            h1_low(1)
            first_norm(3)
            h1_low(2)
            h1_low(3)

            def top16(values, rest, v, ix, keep_apart):
                for t in range(TT):
                    ch.done(V.max(v(t, 0), values(t)))
                ch.wait()
                keep_apart()
                for t in range(TT):
                    ch.done(V.match_replace(out=rest(t), in_to_replace=v(t, 0), in_values=values(t), imm_value=NEG))
                for t in range(TT):
                    ch.done(V.max_index(ix(t, 0), v(t, 0), values(t)))
                ch.wait()
                keep_apart()
                for t in range(TT):
                    ch.done(V.max(v(t, 1), rest(t)))
                ch.wait()
                keep_apart()
                for t in range(TT):
                    ch.done(V.max_index(ix(t, 1), v(t, 1), rest(t)))

            def keep_apart():
                dve.sem_inc(apart, 1)

            with dve.Fori(0, HEADS) as i:
                ch.enter(i, 2 * 21 + 1 + 20 + 4)
                ch.wait()
                for j in range(2):
                    dve.wait_ge(s_free, i * 2 + (j + 3))
                    keep_apart()
                    ch.done(V.tensor_copy(S[:, :, :].rearrange("p t k -> p (t k)"),
                                          S_all[:, bass.ds(i * 2 + j, 1)].rearrange("p a t k -> p (a t k)")))
                    ch.wait()
                    keep_apart()
                    top16(lambda t: S[:, t, :], lambda t: S2[:, t, :],
                          lambda t, k: sv[:, j, t, 8 * k:8 * k + 8], lambda t, k: si[:, j, t, 8 * k:8 * k + 8],
                          keep_apart)
                    ch.wait()
                    keep_apart()
                a0 = sv[:, 0, :, :].unsqueeze(3).to_broadcast([P, TT, TOPK, TOPK])
                a1 = sv[:, 1, :, :].unsqueeze(2).to_broadcast([P, TT, TOPK, TOPK])
                ch.done(V.tensor_tensor(comb[:, :, :, :], a0, a1, ALU.add))
                ch.wait()
                keep_apart()
                flat = comb[:, :, :, :].rearrange("p t a b -> p t (a b)")
                top16(lambda t: flat[:, t, :], lambda t: comb2[:, t, :],
                      lambda t, k: cv[:, t, 8 * k:8 * k + 8], lambda t, k: ci[:, t, 8 * k:8 * k + 8], keep_apart)
                ch.wait()
                keep_apart()
                h = bass.ds(i, 1)
                ch.done(V.tensor_copy(cv_all[:, :, h, :].rearrange("p t a k -> p t (a k)"), cv[:, :, :]))
                ch.done(V.tensor_copy(ci_all[:, :, h, :].rearrange("p t a k -> p t (a k)"), ci[:, :, :]))
                for j in range(2):
                    ch.done(V.tensor_copy(si_all[:, j, :, h, :].rearrange("p t a k -> p t (a k)"), si[:, j, :, :]))
                ch.leave(HEADS)
            ch.wait()
            flat_cv = cv_all[:, :, :, :].rearrange("p t h k -> p (t h) k")
            ch.done(V.tensor_copy(ssum[:, 0, :].unsqueeze(2), flat_cv[:, :, 0:1]))
            ch.wait()
            V.tensor_tensor(flat_cv, flat_cv, ssum[:, 0, :].unsqueeze(2).to_broadcast([P, TT * HEADS, TOPK]),
                            ALU.subtract).then_inc(cmax_ready, 1)
            flat_ci = ci_all[:, :, :, :].rearrange("p t h k -> p (t h k)")
            ch.done(V.tensor_scalar(cdiv[:, 0, :], flat_ci, 4, None, ALU.logical_shift_right))
            ch.done(V.tensor_scalar(cdiv[:, 1, :], flat_ci, TOPK - 1, None, ALU.bitwise_and))
            ch.wait()
            ch.done(V.tensor_copy(cidx[:, :, :], cdiv[:, :, :]))
            ch.wait()
            for k in range(2):
                keys_of = si_all[:, k].rearrange("p t h k -> p (t h) k")
                for j in range(TOPK):
                    ch.done(V.scalar_tensor_tensor(
                        prod[:, j, :].rearrange("p (a k) -> p a k", k=TOPK),
                        cidx[:, k, :].rearrange("p (a k) -> p a k", k=TOPK), float(j),
                        keys_of[:, :, j:j + 1].to_broadcast([P, TT * HEADS, TOPK]), ALU.is_equal, ALU.mult))
                ch.wait()
                ch.done(V.tensor_reduce(sel[:, k, :], prod[:, :, :].rearrange("p j s -> p s j"), AX_X, ALU.add))
                ch.wait()
            dve.wait_ge(cexp_done, 1)
            ch.done(V.tensor_reduce(ssum[:, 0, :], flat_cv, AX_X, ALU.add))
            ch.wait()
            ch.done(V.reciprocal(ssum[:, 1, :], ssum[:, 0, :]))
            ch.wait()
            V.tensor_tensor(sel[:, 2, :].rearrange("p (a k) -> p a k", k=TOPK), flat_cv,
                            ssum[:, 1, :].unsqueeze(2).to_broadcast([P, TT * HEADS, TOPK]),
                            ALU.mult).then_inc(sel_ready, 1)

            dve.wait_ge(selT_ready, 3)
            ch.done(V.tensor_copy(iota4[:, :, :], iota[:, :].unsqueeze(2).to_broadcast([P, KEYS, 4])))
            ch.done(V.tensor_copy(wparts[:, 0, :], selT[:, 2, :]))
            ch.wait()
            ch.done(V.tensor_tensor(wrest[:, :], selT[:, 2, :], wparts[:, 0, :], ALU.subtract))
            ch.wait()
            ch.done(V.tensor_copy(wparts[:, 1, :], wrest[:, :]))
            ch.wait()
            ch.done(V.tensor_tensor(wrest[:, :], wrest[:, :], wparts[:, 1, :], ALU.subtract))
            ch.wait()
            ch.done(V.tensor_copy(wparts[:, 2, :], wrest[:, :]))
            ch.wait()
            dve.sem_inc(oh_ready, 1)

            def per_token(v):
                return v.rearrange("p (a t) -> p a t", t=4).unsqueeze(2).to_broadcast([P, 2, KEYS, 4])

            with dve.Fori(0, WCHUNKS // 2) as i:
                ch.enter(i, 8 * 3)
                for o in range(8):
                    octet = bass.ds(i * 64 + 8 * o, OCT)
                    dve.wait_ge(oh_ready, i * 8 + (o + 1))
                    keep_apart()
                    ch.done(V.tensor_copy(cur[:, :, :], selT[:, 0:2, octet]))
                    ch.wait()
                    dve.wait_ge(quad_done, i * 16 + (2 * o + 2))
                    keys4 = iota4[:, :, :].unsqueeze(1).to_broadcast([P, 2, KEYS, 4])
                    ch.done(V.tensor_tensor(oh1[:, :, :, :], keys4, per_token(cur[:, 0, :]), ALU.is_equal))
                    ch.done(V.tensor_tensor(oh2[:, o % 2, :, :, :], keys4, per_token(cur[:, 1, :]), ALU.is_equal))
                    ch.wait()
                    keep_apart()
                    for part in range(3):
                        ins = V.tensor_tensor(ohw[:, o % 2, part, :, :, :], oh1[:, :, :, :],
                                              per_token(wparts[:, part, octet]), ALU.mult)
                        ins.then_inc(oh_part if part < 2 else oh_ready, 1)
                ch.leave(WCHUNKS // 2)

            def v_low(k, dh):
                dve.wait_ge(v_hi, k * 2 + (dh + 1))
                V.tensor_tensor(vlo[:, dh], vraw[:, dh], vhi[:, dh].bitcast(F32), ALU.subtract).then_inc(v_split, 1)
                dve.wait_ge(v_split, k * 2 + (dh + 1))
                dve.sem_inc(vraw_free[dh], 1)

            def weigh(k, slot, i, blocks, spilled):
                dve.wait_ge(w_in[slot], i * 16 + 16)
                dve.wait_ge(z_free, k * GB + (GB + 2))
                if spilled is not None:
                    dve.wait_ge(g_in[slot], spilled * 16 + 16)
                dve.wait_ge(oe_done, k * 8 + 8)
                V.tensor_tensor(blocks.rearrange("p b (c t) -> p b c t", t=WT),
                                blocks.rearrange("p b (c t) -> p b c t", t=WT),
                                wt[:, slot].rearrange("p c b t -> p b c t"), ALU.mult).then_inc(a_ready, 1)
                dve.wait_ge(a_ready, k + 1)
                dve.sem_inc(w_free[slot], 1)

            def a_low(k, slot, blocks):
                dve.wait_ge(a_hi, k + 1)
                V.tensor_tensor(alo[:, slot], blocks, ahi[:, slot].bitcast(F32), ALU.subtract).then_inc(a_split, 1)

            def sums(k, banks, order, positions):
                for p in positions:
                    dh, t = order[p]
                    dve.wait_ge(oe_done, k * 8 + (p + 17))
                    dve.wait_ge(oe_free, k * 8 + 8)
                    bank = (4 + p) % 8 if banks == 8 else 4 + p % 4
                    cols = slice(dh * HD, (dh + 1) * HD)
                    V.tensor_tensor(htok[:, t, cols], htok[:, t, cols], ps[:, bank, :], ALU.add).then_inc(oe_free, 1)

            FIRST_HALF, SECOND_HALF = range(TT), range(TT, 2 * TT)

            def step(k, nxt=None):
                if nxt is not None:
                    n, slot, use, first_block, spilled = nxt
                    blocks = G[:, first_block:first_block + GB, :]
                    weigh(n, slot, use, blocks, spilled)
                    a_low(n, slot, blocks)
                for dh in range(2):
                    sums(k, 8, BY_HALF, (FIRST_HALF, SECOND_HALF)[dh])
                    if nxt is not None:
                        v_low(n, dh)

            dve.wait_ge(acc_ready, TT)
            dve.wait_ge(w_stored[0], 16 * (WCHUNKS // 2 + 1))
            dve.wait_ge(w_stored[1], 16 * (WCHUNKS // 2 + 1))
            v_low(0, 0)
            v_low(0, 1)
            weigh(0, 0, 0, G[:, 0:GB, :], None)
            a_low(0, 0, G[:, 0:GB, :])
            for k in range(1, AHEAD + 1):
                step(k - 1, (k, k % 2, k // 2, k * GB if k < AHEAD else 0, None if k < AHEAD else 0))
            with dve.Fori(0, SPILLED // 2 - 1) as i:
                step(i * 2 + AHEAD, (i * 2 + (AHEAD + 1), 1, i + AHEAD // 2, GB, i))
                step(i * 2 + (AHEAD + 1), (i * 2 + (AHEAD + 2), 0, i + (AHEAD // 2 + 1), 0, i + 1))
            step(FIRST - 2, (FIRST - 1, 1, FIRST // 2 - 1, GB, SPILLED // 2 - 1))
            step(FIRST - 1)

            def pair(k, i, finish=None):
                v_low(k, 0)
                v_low(k, 1)
                for s in range(2):
                    blocks = G[:, s * GB:(s + 1) * GB, :]
                    weigh(k + s, s, i + FIRST // 2, blocks, None)
                    a_low(k + s, s, blocks)
                sums(k, 4, BY_HALF, FIRST_HALF)
                v_low(k + 1, 0)
                sums(k, 4, BY_HALF, SECOND_HALF)
                v_low(k + 1, 1)
                for p, (dh, t) in enumerate(BY_TILES):
                    sums(k + 1, 4, BY_TILES, (p,))
                    if finish is not None and dh == 1:
                        finish(t, p)

            def last_norm(t, p):
                if t == 0:
                    dve.wait_ge(ln2_in, 32)
                dve.wait_ge(oe_free, 8 * GROUPS + p + 1)
                norm_stats(htok[:, t, :], P, t)
                ch.wait()
                V.tensor_scalar(veps[:, t:t + 1], mv[:, t, 1:2], EPS, None, ALU.add).then_inc(var_ready, 1)
                dve.wait_ge(sd_ready, SD + TT + t + 1)
                ch.done(V.reciprocal(rstd[:, t:t + 1], sdev[:, t:t + 1]))
                ch.wait()
                norm_apply(htok[:, t, :], P, t, ln2bc, out_ready)

            pairs = (GROUPS - FIRST) // 2
            with dve.Fori(0, pairs - 1) as i:
                pair(i * 2 + FIRST, i)
            pair(GROUPS - 2, pairs - 1, last_norm)


def kernel(x, meta, ln_in_g, ln_in_b, w_in, conv_w, conv_b, w_rg, b_rg, w_ig, b_ig, lru_L,
           w_proj_a, pool_w, pool_scale, w_proj_b, w_out, ln1_g, ln1_b, w_q, sub_keys,
           expert_u, expert_v, ln2_g, ln2_b):
    import numpy as np
    import concourse.bacc as bacc
    from concourse.bass_utils import run_bass_kernel_spmd

    nc = bacc.Bacc("TRN2", target_bir_lowering=False, num_devices=1)
    arrays, args = {}, []

    def give(name, a):
        a = np.ascontiguousarray(a)
        arrays[name] = a
        args.append(nc.dram_tensor(name, a.shape, mybir.dt.from_np(a.dtype), kind="ExternalInput").ap())

    def columns(v):
        return np.asarray(v).reshape(-1, P).T

    def stationary(w):
        w = np.asarray(w)
        k, n = w.shape
        return w.reshape(k // P, P, n // P, P).transpose(2, 1, 0, 3).reshape(n // P, P, k)

    w = np.asarray(w_in)[0]
    n_pool = POOL_C * P
    give("x_d", np.asarray(x).reshape(TT, P, D))
    give("meta_d", meta)
    give("ln_d", np.stack([np.asarray(v).reshape(-1) for v in (ln_in_g, ln_in_b, ln1_g, ln1_b, ln2_g, ln2_b)]))
    cw = np.asarray(conv_w)[0].reshape(CONV, C, P).transpose(2, 1, 0).reshape(P, C * CONV)
    give("par_d", np.concatenate([cw, columns(conv_b), columns(b_rg), columns(b_ig), columns(lru_L),
                                  columns(pool_scale)], axis=1))
    give("ident_d", np.eye(P, dtype=np.float32))
    give("iota_d", np.tile(np.arange(P, dtype=np.float32), (P, 1)))
    give("wxr_d", stationary(w[:, 0:D]))
    give("wxp_d", stationary(w[:, 2 * D:2 * D + n_pool]))
    give("wga_d", stationary(w[:, D:2 * D]))
    give("wgl_d", stationary(w[:, 2 * D + n_pool:]))
    gw = np.stack([np.asarray(w_rg)[0], np.asarray(w_ig)[0]], axis=1)
    give("wrgig_d", gw.reshape(4, 2, 2, P, 256).transpose(0, 3, 1, 2, 4).reshape(4, P, D))
    give("poolw_d", np.asarray(pool_w)[0].transpose(1, 0, 2).reshape(P, POOL_GROUPS * P))
    give("wpa_d", stationary(np.asarray(w_proj_a)[0]))
    give("wpb_d", stationary(np.asarray(w_proj_b)[0]).reshape(C // 2, 2, P, HD).transpose(0, 2, 1, 3)
         .reshape(C // 2, P, D))
    give("wo_d", np.asarray(w_out)[0].reshape(C, P, D))
    give("wq_d", stationary(np.asarray(w_q)[0]))
    give("keys_d", np.asarray(sub_keys)[0].reshape(2 * HEADS, KEYS, P).transpose(2, 0, 1))
    give("u_d", np.asarray(expert_u)[0].reshape(KEYS, P, C, P).transpose(0, 3, 2, 1).reshape(KEYS, P, D))
    give("v_d", np.asarray(expert_v)[0].reshape(GROUPS, GB, P, 2, HD).transpose(0, 3, 2, 1, 4)
         .reshape(2 * GROUPS, P, GB * HD))
    out = nc.dram_tensor("out_d", (TT, P, D), F32, kind="ExternalOutput")
    layer(nc, *args, out.ap())
    r = run_bass_kernel_spmd(nc, [arrays], core_ids=[0])
    return r.results[0]["out_d"].reshape(1, N, D)
```
